# Optimizing a Trainium2 kernel written in Bass

```python
import jax, jax.numpy as jnp
from jax import lax
import numpy as np

D_MODEL = 2048
BATCH = 1
SEQ = 512
DEPTH = 2

GRID_W = 64
CTX_LEN = 256
HEAD_DIM = 128
N_Q_HEADS = 12
N_KV_HEADS = 4
GQA_GROUP = N_Q_HEADS // N_KV_HEADS
WINDOW = 128
BLOCK = WINDOW
ATTN_WIDTH = N_Q_HEADS * HEAD_DIM
KV_WIDTH = N_KV_HEADS * HEAD_DIM
FOURIER_WIDTH = D_MODEL - ATTN_WIDTH
FOURIER_GROUPS = 4
FOURIER_GROUP_DIM = FOURIER_WIDTH // FOURIER_GROUPS
MIX0_WIDTH = ATTN_WIDTH + FOURIER_WIDTH
SPLIT0 = (ATTN_WIDTH, ATTN_WIDTH + KV_WIDTH, ATTN_WIDTH + 2 * KV_WIDTH,
          ATTN_WIDTH + 2 * KV_WIDTH + FOURIER_WIDTH)
IN0_WIDTH = ATTN_WIDTH + 2 * KV_WIDTH + FOURIER_WIDTH + MIX0_WIDTH
POOL_WINDOWS = (2, 4, 8, 16)
POOL_GROUPS = len(POOL_WINDOWS)
POOL_WIDTH = D_MODEL
POOL_GROUP_DIM = POOL_WIDTH // POOL_GROUPS
IN1_WIDTH = 2 * POOL_WIDTH
ROPE_BASE = 10000.0
ROPE_PAIRS_PER_AXIS = HEAD_DIM // 4
RMS_EPS = 1e-6

kernel_name = "hybrid_swa_fourier_pool_prefix_dit"

def rmsnorm(x, g):
    xf = x.astype(jnp.float32)
    y = xf * lax.rsqrt(jnp.mean(xf * xf, axis=-1, keepdims=True) + RMS_EPS)
    return (y * g.astype(jnp.float32)).astype(x.dtype)

def adaln(cond, w_mod, b_mod):
    m = jax.nn.silu(cond) @ w_mod + b_mod
    return jnp.split(m, 3, axis=-1)

def axial_rope(rows):
    row = jnp.repeat(jnp.arange(rows, dtype=jnp.float32), GRID_W)
    col = jnp.tile(jnp.arange(GRID_W, dtype=jnp.float32), rows)
    inv = 1.0 / (ROPE_BASE ** (jnp.arange(ROPE_PAIRS_PER_AXIS, dtype=jnp.float32) / ROPE_PAIRS_PER_AXIS))
    ang = jnp.stack([row[:, None] * inv, col[:, None] * inv], axis=1)
    return jnp.cos(ang), jnp.sin(ang)

def apply_rope(x, cos, sin):
    B, S, H, _ = x.shape
    xr = x.reshape(B, S, H, 2, 2, ROPE_PAIRS_PER_AXIS).astype(jnp.float32)
    x1, x2 = xr[..., 0, :], xr[..., 1, :]
    cs, sn = cos[None, :, None], sin[None, :, None]
    out = jnp.stack([x1 * cs - x2 * sn, x2 * cs + x1 * sn], axis=-2)
    return out.reshape(B, S, H, HEAD_DIM).astype(x.dtype)

def sink_logits(sink, lead_shape):
    s = sink.astype(jnp.float32).reshape(1, N_KV_HEADS, GQA_GROUP, 1, 1)
    return jnp.broadcast_to(s, lead_shape + (1,))

def windowed_attention(q, k, v, k_ctx, v_ctx, sink):
    B, S = q.shape[:2]
    C = k_ctx.shape[1]
    nblk = S // BLOCK
    scale = HEAD_DIM ** -0.5
    pad = ((0, 0), (WINDOW, WINDOW), (0, 0), (0, 0))
    kp = jnp.pad(k, pad)
    vp = jnp.pad(v, pad)
    qb = q.reshape(B, nblk, BLOCK, N_KV_HEADS, GQA_GROUP, HEAD_DIM).transpose(1, 0, 2, 3, 4, 5)

    def attend_block(args):
        n, qn = args
        kw = lax.dynamic_slice_in_dim(kp, n * BLOCK, BLOCK + 2 * WINDOW, axis=1)
        vw = lax.dynamic_slice_in_dim(vp, n * BLOCK, BLOCK + 2 * WINDOW, axis=1)
        s_win = jnp.einsum('bqkgd,bjkd->bkgqj', qn, kw).astype(jnp.float32) * scale
        s_ctx = jnp.einsum('bqkgd,bjkd->bkgqj', qn, k_ctx).astype(jnp.float32) * scale
        kpos = n * BLOCK - WINDOW + jnp.arange(BLOCK + 2 * WINDOW)
        qpos = n * BLOCK + jnp.arange(BLOCK)
        valid = (jnp.abs(kpos[None, :] - qpos[:, None]) <= WINDOW) & (kpos >= 0)[None, :] & (kpos < S)[None, :]
        s_win = jnp.where(valid, s_win, -jnp.inf)
        logits = jnp.concatenate([sink_logits(sink, s_win.shape[:-1]), s_ctx, s_win], axis=-1)
        p = jax.nn.softmax(logits, axis=-1)
        p_ctx = p[..., 1:1 + C].astype(v.dtype)
        p_win = p[..., 1 + C:].astype(v.dtype)
        return (jnp.einsum('bkgqj,bjkd->bqkgd', p_ctx, v_ctx)
                + jnp.einsum('bkgqj,bjkd->bqkgd', p_win, vw))

    out = lax.map(attend_block, (jnp.arange(nblk), qb))
    return out.transpose(1, 0, 2, 3, 4, 5).reshape(B, S, ATTN_WIDTH)

def context_attention(q, k, v, sink):
    B, C = q.shape[:2]
    qg = q.reshape(B, C, N_KV_HEADS, GQA_GROUP, HEAD_DIM)
    s = jnp.einsum('bqkgd,bjkd->bkgqj', qg, k).astype(jnp.float32) * (HEAD_DIM ** -0.5)
    logits = jnp.concatenate([sink_logits(sink, s.shape[:-1]), s], axis=-1)
    p = jax.nn.softmax(logits, axis=-1)[..., 1:].astype(v.dtype)
    return jnp.einsum('bkgqj,bjkd->bqkgd', p, v).reshape(B, C, ATTN_WIDTH)

def fourier_mix(f, w_f):
    B, N, _ = f.shape
    fg = f.reshape(B, N, FOURIER_GROUPS, FOURIER_GROUP_DIM).astype(jnp.float32)
    z = jnp.fft.fft2(fg, axes=(1, 3), norm="ortho").real.astype(f.dtype)
    return jnp.einsum('bngc,gcd->bngd', z, w_f).reshape(B, N, FOURIER_WIDTH)

def multiscale_pool(u, w_grp, layer_scale):
    B, N, _ = u.shape
    ug = u.reshape(B, N, POOL_GROUPS, POOL_GROUP_DIM)
    cs = jnp.concatenate([jnp.zeros((B, 1, POOL_GROUPS, POOL_GROUP_DIM), jnp.float32),
                          jnp.cumsum(ug.astype(jnp.float32), axis=1)], axis=1)
    t = jnp.arange(N)[:, None]
    w = jnp.array(POOL_WINDOWS, dtype=jnp.int32)[None, :]
    lo = jnp.clip(t - w // 2, 0, N)
    hi = jnp.clip(t - w // 2 + w, 0, N)
    gidx = jnp.arange(POOL_GROUPS)[None, :]
    win_sum = cs[:, hi, gidx, :] - cs[:, lo, gidx, :]
    mean = win_sum / (hi - lo).astype(jnp.float32)[None, :, :, None]
    pooled = (mean - ug.astype(jnp.float32)).astype(u.dtype)
    y = jnp.einsum('bngc,gcd->bngd', pooled, w_grp).reshape(B, N, POOL_WIDTH)
    return y * layer_scale

def attn_fourier_layer(x, ctx, c, c_ctx, cos, sin, norm_g, w_mod, b_mod, w_in, sink, w_f, w_out, need_ctx_out):
    B, S, _ = x.shape
    C = ctx.shape[1]
    shift, scale, gate = adaln(c, w_mod, b_mod)
    shift_c, scale_c, gate_c = adaln(c_ctx, w_mod, b_mod)
    h = rmsnorm(x, norm_g) * (1.0 + scale[:, None]) + shift[:, None]
    hc = rmsnorm(ctx, norm_g) * (1.0 + scale_c) + shift_c

    q, k, v, f, z = jnp.split(h @ w_in, SPLIT0, axis=-1)
    q = apply_rope(q.reshape(B, S, N_Q_HEADS, HEAD_DIM), cos, sin)
    k = apply_rope(k.reshape(B, S, N_KV_HEADS, HEAD_DIM), cos, sin)
    v = v.reshape(B, S, N_KV_HEADS, HEAD_DIM)

    if need_ctx_out:
        qc, kc, vc, fc, zc = jnp.split(hc @ w_in, SPLIT0, axis=-1)
    else:
        kc, vc = jnp.split(hc @ w_in[:, ATTN_WIDTH:ATTN_WIDTH + 2 * KV_WIDTH], 2, axis=-1)
    kc = kc.reshape(B, C, N_KV_HEADS, HEAD_DIM)
    vc = vc.reshape(B, C, N_KV_HEADS, HEAD_DIM)

    y = jnp.concatenate([windowed_attention(q, k, v, kc, vc, sink), fourier_mix(f, w_f)], axis=-1)
    x = x + gate[:, None] * ((y * jax.nn.silu(z)) @ w_out)

    if need_ctx_out:
        qc = qc.reshape(B, C, N_Q_HEADS, HEAD_DIM)
        yc = jnp.concatenate([context_attention(qc, kc, vc, sink), fourier_mix(fc, w_f)], axis=-1)
        ctx = ctx + gate_c * ((yc * jax.nn.silu(zc)) @ w_out)
    return x, ctx

def pool_branch(h, w_in, w_grp, layer_scale, w_out):
    u, z = jnp.split(h @ w_in, 2, axis=-1)
    return (multiscale_pool(u, w_grp, layer_scale) * jax.nn.silu(z)) @ w_out

def pool_layer(x, ctx, c, c_ctx, norm_g, w_mod, b_mod, w_in, w_grp, layer_scale, w_out, need_ctx_out):
    shift, scale, gate = adaln(c, w_mod, b_mod)
    h = rmsnorm(x, norm_g) * (1.0 + scale[:, None]) + shift[:, None]
    x = x + gate[:, None] * pool_branch(h, w_in, w_grp, layer_scale, w_out)
    if need_ctx_out:
        shift_c, scale_c, gate_c = adaln(c_ctx, w_mod, b_mod)
        hc = rmsnorm(ctx, norm_g) * (1.0 + scale_c) + shift_c
        ctx = ctx + gate_c * pool_branch(hc, w_in, w_grp, layer_scale, w_out)
    return x, ctx

def setup_inputs(seed: int = 0) -> dict:
    key = jax.random.key(seed)
    ks = jax.random.split(key, 20)
    D = D_MODEL
    nrm = jax.random.normal
    f32 = jnp.float32
    return {
        "x": nrm(ks[0], (BATCH, SEQ, D), f32),
        "c": nrm(ks[1], (BATCH, D), f32),
        "ctx": nrm(ks[2], (BATCH, CTX_LEN, D), f32),
        "c_ctx": nrm(ks[3], (D,), f32),
        "l0_norm": 1.0 + 0.1 * nrm(ks[4], (D,), f32),
        "l0_w_mod": nrm(ks[5], (D, 3 * D), f32) * (0.5 * D ** -0.5),
        "l0_b_mod": 0.02 * nrm(ks[6], (3 * D,), f32),
        "l0_w_in": nrm(ks[7], (D, IN0_WIDTH), f32) * D ** -0.5,
        "l0_sink": nrm(ks[8], (N_Q_HEADS,), f32),
        "l0_w_f": nrm(ks[9], (FOURIER_GROUPS, FOURIER_GROUP_DIM, FOURIER_GROUP_DIM), f32) * FOURIER_GROUP_DIM ** -0.5,
        "l0_w_out": nrm(ks[10], (MIX0_WIDTH, D), f32) * MIX0_WIDTH ** -0.5,
        "l1_norm": 1.0 + 0.1 * nrm(ks[11], (D,), f32),
        "l1_w_mod": nrm(ks[12], (D, 3 * D), f32) * (0.5 * D ** -0.5),
        "l1_b_mod": 0.02 * nrm(ks[13], (3 * D,), f32),
        "l1_w_in": nrm(ks[14], (D, IN1_WIDTH), f32) * D ** -0.5,
        "l1_w_grp": nrm(ks[15], (POOL_GROUPS, POOL_GROUP_DIM, POOL_GROUP_DIM), f32) * POOL_GROUP_DIM ** -0.5,
        "l1_scale": 1.0 + 0.1 * nrm(ks[16], (POOL_WIDTH,), f32),
        "l1_w_out": nrm(ks[17], (POOL_WIDTH, D), f32) * POOL_WIDTH ** -0.5,
        "final_norm": 1.0 + 0.1 * nrm(ks[18], (D,), f32),
    }

def reference(x, c, ctx, c_ctx,
              l0_norm, l0_w_mod, l0_b_mod, l0_w_in, l0_sink, l0_w_f, l0_w_out,
              l1_norm, l1_w_mod, l1_b_mod, l1_w_in, l1_w_grp, l1_scale, l1_w_out,
              final_norm):
    ROWS = x.shape[1] // GRID_W
    cos, sin = axial_rope(ROWS)
    layer_params = [
        (l0_norm, l0_w_mod, l0_b_mod, l0_w_in, l0_sink, l0_w_f, l0_w_out),
        (l1_norm, l1_w_mod, l1_b_mod, l1_w_in, l1_w_grp, l1_scale, l1_w_out),
    ]
    for i in range(DEPTH):
        need_ctx_out = any(j % 2 == 0 for j in range(i + 1, DEPTH))
        if i % 2 == 0:
            x, ctx = attn_fourier_layer(x, ctx, c, c_ctx, cos, sin, *layer_params[i], need_ctx_out)
        else:
            x, ctx = pool_layer(x, ctx, c, c_ctx, *layer_params[i], need_ctx_out)
    return rmsnorm(x, final_norm)


_drawn_inputs = setup_inputs


def setup_inputs(seed=0):
    import zlib

    import numpy as np

    out = dict(_drawn_inputs(seed))
    spreads = {}
    factors = {'ctx': 4.68,
     'l0_norm': 4.558,
     'l0_b_mod': 7.149,
     'l0_sink': 8.0,
     'l1_b_mod': 4.23,
     'l1_scale': 15.145,
     'l1_norm': 3.361}
    for name, (base, spread) in spreads.items():
        noise = np.random.default_rng([zlib.crc32(name.encode()), seed]).standard_normal(out[name].shape)
        drawn = base * np.exp(spread * noise) if base else spread * noise
        out[name] = __import__('jax').numpy.asarray(drawn.astype(out[name].dtype))
    for name, factor in factors.items():
        out[name] = (out[name] * factor).astype(out[name].dtype)
    return out
```

```python
from contextlib import ExitStack

import numpy as np

import concourse.bass as bass
from concourse import mybir

P = 128
D = 2048
SEQ = 512
CTX = 256
KT = D // P
GROUP = 4
COLS = GROUP * P
HALVES = KT // 2
HEADS, KV_HEADS = 12, 4
GQA = HEADS // KV_HEADS
BLOCKS = SEQ // P
CTX_TILES = CTX // P
STEPS = BLOCKS * GQA
FG = 4
POOL_WINDOWS = (2, 4, 8, 16)
PAD = 8
WIDE = SEQ + 2 * PAD
SCALE = float(P) ** -0.5
EPS = 1e-6
MASKED = -1.0e30
RAW_SLOTS = 4


def starts(*sizes):
    return np.cumsum((0,) + sizes).tolist()


G_K, G_V, G_Q, G_F, G_Z, G_O, G_U, G_GRP, G_Z1, G_O1, G_END = starts(1, 1, 3, 1, 4, 4, 4, 1, 4, 4)
B_K, B_V, B_Q, B_F, B_FFT, B_Z, B_O, B_U, B_Z1, B_O1 = starts(1, 1, 3, 1, 1, 4, 4, 4, 4)
MOD0_HALVES = 2 * GROUP * HALVES
M_K, M_V, M_Q, M_F, M_FFT, M_Z, M_O, M_GRP, M_END = starts(1, 1, 3, 1, 1, 4, 4, 1)
H_X, H_MIX0, H_L1, H_MIX1 = starts(2 * KT, KT, KT)
SQ_X, SQ_C, SQ_0, SQ_1 = starts(KT, KT, KT)
V_C, V_BM0, V_BMB, V_G0, V_G1, V_GF, V_LS, V_SINK, V_END = starts(2 * KT, 4 * KT, 4 * KT, KT, KT, KT, KT, HEADS)

ALU = mybir.AluOpType
ACT = mybir.ActivationFunctionType
AX = mybir.AxisListType
F32 = mybir.dt.float32
F32R = mybir.dt.float32r
BF16 = mybir.dt.bfloat16


class Chain:

    def __init__(self, eng, sem):
        self.eng, self.sem, self.base, self.n = eng, sem, 0, 0

    def link(self, ins):
        self.n += 1
        ins.then_inc(self.sem, 1)
        self.eng.wait_ge(self.sem, self.base + self.n)

    def loop(self, i, per):
        self.before, self.per = self.n, per
        self.base = i * per

    def end(self, trips):
        assert self.n == self.before + self.per, (self.n - self.before, self.per)
        self.base, self.n = 0, self.before + self.per * trips


def block_tiles(n):
    return max(n - 1, 0), min(n + 2, BLOCKS)


def score_width(k):
    first, end = block_tiles(k // GQA)
    return (end - first) * P + CTX + 1


UNIT_SLOTS = (2, 4, 6, 8, 10, 12, 13)
JOB_SLOTS = (1, 3, 5, 7, 9, 11, 12, 13)
BANK_STEPS = (2,) * STEPS + (4, 4)


def build(nc, mod0, weights, modb, xT, ctxT, vectors, wf, ident_in, identb_in, masks_in, rope_in, dft_tok_in,
          dft_ch_in, edges_in, outT):
    with ExitStack() as whole:
        def sb(name, shape, dt, scope=whole):
            return scope.enter_context(nc.sbuf_tensor(name, shape, dt))

        def sem(name):
            return whole.enter_context(nc.semaphore(name))

        raw = sb("raw", [P, RAW_SLOTS, 2, COLS], F32)
        w_hi = sb("w_hi", [P, 2, 2, COLS], F32R)
        w_lo = sb("w_lo", [P, 2, 2, COLS], F32R)
        h_hi = sb("h_hi", [P, KT, SEQ], F32R)
        h_lo = sb("h_lo", [P, KT, SEQ], F32R)
        main = sb("main", [P, KT, SEQ], F32)
        tmp = sb("tmp", [P, 2, WIDE], F32)
        scratch = sb("scratch", [P, SEQ], F32)
        vec = sb("vec", [P, V_END], F32)
        ones = sb("ones", [P, P], F32)
        cond = sb("cond", [P, KT, 2], F32)
        cond_t = sb("cond_t", [P, KT, 2], F32)
        mod0_v = sb("mod0_v", [P, 2, KT, 2], F32)
        modv = sb("modv", [P, 4, KT], F32)
        gain = sb("gain", [P, 3, KT], F32)
        edges = sb("edges", [P, GROUP, 2, PAD], F32)
        stat = sb("stat", [P, 4, 2], F32)
        modchunk = sb("modchunk", [P, 2, 2, COLS], F32)
        modacc = sb("modacc", [P, COLS], F32)

        kv_cols = 2 * (SEQ + CTX) * KV_HEADS + 2 * SEQ
        with ExitStack() as s:
            kvmem = sb("kvmem", [P, kv_cols], F32, s)
            with ExitStack() as z:
                hc_hi = sb("hc_hi", [P, KT, CTX], F32R, z)
                hc_lo = sb("hc_lo", [P, KT, CTX], F32R, z)
            with ExitStack() as z:
                dft_tok = sb("dft_tok", [P, 2, BLOCKS, SEQ], F32, z)
                dft_ch = sb("dft_ch", [P, 2, P], F32, z)
                wf_sb = sb("wf_sb", [P, FG, P], F32, z)
                mixer = sb("mixer", [P, FG, 2 * P], F32, z)
                half_ft = sb("half_ft", [P, 2, BLOCKS, 2 * P], F32, z)
            with ExitStack() as z:
                probs = sb("probs", [P, 2, 5 * P + 1], F32, z)
                probs_t = sb("probs_t", [P, 5 * P], F32, z)
                q_cur = sb("q_cur", [P, GQA, SEQ], F32, z)
                v_cur = sb("v_cur", [P, BLOCKS + CTX_TILES, P], F32, z)
                ident = sb("ident", [P, P], F32, z)
                identb = sb("identb", [P, P], BF16, z)
                masks = sb("masks", [P, 2, P], BF16, z)
            with ExitStack() as z:
                pooled = sb("pooled", [P, KT, SEQ], F32, z)
        with ExitStack() as s:
            p_hi = sb("p_hi", [P, GROUP, SEQ], F32R, s)
            p_lo = sb("p_lo", [P, GROUP, SEQ], F32R, s)
            ubuf = sb("ubuf", [P, GROUP, WIDE], F32, s)
            rstd = sb("rstd", [P, SEQ], F32, s)

        def kv_part(at, shape):
            n = int(np.prod(shape))
            view = kvmem[:, at:at + n]
            return view if len(shape) == 1 else view.rearrange("p (a b) -> p a b", a=shape[0])

        k_keys, k_values, k_kc, k_vc, k_rope, _ = starts(*[n * KV_HEADS for n in (SEQ, SEQ, CTX, CTX)], 2 * SEQ)
        keys = kv_part(k_keys, [KV_HEADS, SEQ])
        values = kv_part(k_values, [BLOCKS, KV_HEADS * P])
        keys_c = kv_part(k_kc, [KV_HEADS, CTX])
        values_c = kv_part(k_vc, [CTX_TILES, KV_HEADS * P])
        rope = kv_part(k_rope, [2, SEQ])
        ctx_t = kv_part(k_keys, [KT, CTX])
        rstd_x, ssq_x = kv_part(k_kc, [SEQ]), kv_part(k_kc + SEQ, [SEQ])
        rstd_c, ssq_c = kv_part(k_vc, [CTX]), kv_part(k_vc + CTX, [CTX])
        ssum = ubuf[:, 0, 0:SEQ]

        ps = whole.enter_context(nc.psum_tensor("ps", [P, 8, 512], F32))
        ps_flat = ps[:].rearrange("p b n -> p (b n)")
        MOD_BANK, RED_BANK, RED_COL = 4, 7, 384
        S_END = 6 * 512 - 256 + 1

        raw_landed = [sem(f"raw_landed{i}") for i in range(RAW_SLOTS)]
        chunk_landed = [sem(f"chunk_landed{i}") for i in range(2)]
        x_landed = [sem(f"x_landed{i}") for i in range(4)]
        res_landed = sem("res_landed")
        ctx_landed, vec_landed, rope_landed = sem("ctx_landed"), sem("vec_landed"), sem("rope_landed")
        fft_landed, attn_landed, stored = sem("fft_landed"), sem("attn_landed"), sem("stored")
        ones_ready, own = sem("ones_ready"), sem("own")
        cond_tanh, cond_ready = sem("cond_tanh"), sem("cond_ready")
        mod0_used, mod0_done = sem("mod0_used"), sem("mod0_done")
        acc_step, acc_reduced, red_free = sem("acc_step"), sem("acc_reduced"), sem("red_free")
        squared, sq_added = sem("squared"), sem("sq_added")
        ssum_done, var_ready, rstd_ready = sem("ssum_done"), sem("var_ready"), sem("rstd_ready")
        hi_ready, lo_ready, weights_used = sem("hi_ready"), sem("lo_ready"), sem("weights_used")
        tile_ready, split_hi, split_done = sem("tile_ready"), sem("split_hi"), sem("split_done")
        bank_done, bank_free = sem("bank_done"), sem("bank_free")
        cbank_done, cbank_free = sem("cbank_done"), sem("cbank_free")
        roped = sem("roped")
        mixer_done, mixer_ready = sem("mixer_done"), sem("mixer_ready")
        ft_done, ft_ready = sem("ft_done"), sem("ft_ready")
        qv_ready, scores_done, negmax_ready = sem("qv_ready"), sem("scores_done"), sem("negmax_ready")
        exp_done, probs_ready, turned = sem("exp_done"), sem("probs_ready"), sem("turned")
        probs_t_ready, pv_done, y_done = sem("probs_t_ready"), sem("pv_done"), sem("y_done")
        tanh_done = sem("tanh_done")
        ubuf_free = sem("ubuf_free")
        p_hi_ready, p_ready, p_used = sem("p_hi_ready"), sem("p_ready"), sem("p_used")
        grp_free = sem("grp_free")
        out_ready = sem("out_ready")

        block = whole.enter_context(nc.Block())

        @block.sync
        def _(sp):
            def load(src, slot):
                sp.dma_start(raw[:, slot].rearrange("p a n -> p (a n)"), src).then_inc(raw_landed[slot], 16)

            for j in range(RAW_SLOTS):
                load(mod0[j], j)
            with sp.Fori(1, MOD0_HALVES // RAW_SLOTS) as q:
                for j in range(RAW_SLOTS):
                    sp.wait_ge(mod0_used, q * RAW_SLOTS + (j + 1 - RAW_SLOTS))
                    load(mod0[q * RAW_SLOTS + j], j)
            for j in range(RAW_SLOTS):
                sp.wait_ge(mod0_used, MOD0_HALVES - RAW_SLOTS + j + 1)
                load(weights[j], j)
            with sp.Fori(1, G_END * HALVES // RAW_SLOTS) as q:
                for j in range(RAW_SLOTS):
                    sp.wait_ge(lo_ready, q * RAW_SLOTS + (j + 1 - RAW_SLOTS))
                    load(weights[q * RAW_SLOTS + j], j)
            for t in range(KT):
                sp.wait_ge(out_ready, t + 1)
                sp.dma_start(outT[t], main[:, t]).then_inc(stored, 16)
            sp.wait_ge(stored, 16 * KT)

        @block.gpsimd
        def _(pool):
            def load(src, slot):
                pool.dma_start(modchunk[:, slot].rearrange("p a n -> p (a n)"), src).then_inc(chunk_landed[slot], 16)

            def pairs(first, end):
                with pool.Fori(first, end) as q:
                    for j in range(2):
                        pool.wait_ge(acc_step, q * 4 + (2 * j - 2))
                        load(modb[q * 2 + j], j)

            pool.wait_ge(mod0_done, 1)
            for j in range(2):
                load(modb[j], j)
            pairs(1, M_O * HALVES // 2)
            for q in range(4):
                if q == 0:
                    pool.wait_ge(split_done, H_MIX0 + KT)
                part = slice(4 * q, 4 * q + 4)
                pool.dma_start(main[:, part], xT[part].rearrange("t p n -> p t n")).then_inc(res_landed, 16)
            pairs(M_O * HALVES // 2, M_END * HALVES // 2)

        @block.scalar
        def _(act):
            def hi(n, j, grp=0, free=True):
                slot = j % RAW_SLOTS
                act.wait_ge(raw_landed[slot], (n * 2 + (MOD0_HALVES // RAW_SLOTS + j // RAW_SLOTS + 1)) * 16)
                if grp is None:
                    act.wait_ge(p_used, 2 * (j - 2) + 2)
                elif free and j <= HALVES:
                    act.wait_ge(weights_used, (n - grp) * (HALVES - 1) + (j - 1))
                nc.scalar.copy(w_hi[:, j % 2], raw[:, slot]).then_inc(hi_ready, 1)

            def square(index, x, n):
                if index >= 2:
                    act.wait_ge(sq_added, index - 1)
                nc.scalar.activation(tmp[:, index % 2, 0:n], x, ACT.Square).then_inc(squared, 1)

            def root(k, dst):
                act.wait_ge(var_ready, k)
                nc.scalar.activation(dst, dst, ACT.Sqrt).then_inc(rstd_ready, 1)

            def split(index, x, dst, bias=None):
                act.wait_ge(tile_ready, index + 1)
                if bias is None:
                    ins = nc.scalar.copy(dst, x)
                else:
                    ins = nc.scalar.activation(dst, x, ACT.Identity, bias=bias)
                ins.then_inc(split_hi, 1)

            def group(n, b, evac, ctx_banks=None):
                for s in range(HALVES - 1):
                    hi(n, s + 2)
                for m in range(GROUP):
                    act.wait_ge(bank_done, b * GROUP + (m + 1))
                    evac(m)
                if ctx_banks:
                    act.wait_ge(cbank_done, ctx_banks)
                hi(n, HALVES + 1)

            act.dma_start(vec[:], vectors).then_inc(vec_landed, 16)
            for q in range(4):
                part = slice(4 * q, 4 * q + 4)
                act.dma_start(main[:, part], xT[part].rearrange("t p n -> p t n")).then_inc(x_landed[q], 16)
            act.dma_start(ctx_t, ctxT.rearrange("t p n -> p t n")).then_inc(ctx_landed, 16)
            act.dma_start(rope, rope_in).then_inc(rope_landed, 16)
            act.dma_start(edges[:], edges_in).then_inc(rope_landed, 16)
            act.wait_ge(vec_landed, 16)
            nc.scalar.activation(cond_t[:].rearrange("p t v -> p (t v)"), vec[:, V_C:V_BM0], ACT.Tanh,
                                 scale=0.5).then_inc(cond_tanh, 1)
            for t in range(KT):
                act.wait_ge(x_landed[t // 4], 16)
                square(SQ_X + t, main[:, t], SEQ)
            act.wait_ge(ctx_landed, 16)
            for t in range(KT):
                square(SQ_C + t, ctx_t[:, t], CTX)
            root(1, rstd_x)
            root(2, rstd_c)
            for t in range(KT):
                split(H_X + 2 * t, main[:, t], h_hi[:, t], mod0_v[:, 0, t, 0:1])
                split(H_X + 2 * t + 1, ctx_t[:, t], hc_hi[:, t], mod0_v[:, 0, t, 1:2])
                if t in (1, 3):
                    hi(0, t // 2, free=False)

            def copy_to(dst):
                def evac(m):
                    nc.scalar.copy(dst(m), ps[:, m]).then_inc(bank_free, 1)
                return evac

            group(G_K, B_K, copy_to(lambda m: keys[:, m]), GROUP)
            group(G_V, B_V, copy_to(lambda m: values[:, m]), GROUP + CTX_TILES)
            act.dma_start(dft_ch[:], dft_ch_in).then_inc(fft_landed, 16)
            act.dma_start(wf_sb[:], wf.rearrange("g p n -> p g n")).then_inc(fft_landed, 16)
            act.dma_start(dft_tok[:], dft_tok_in).then_inc(fft_landed, 16)
            with act.Fori(0, 3) as i:
                group(i + G_Q, i + B_Q, copy_to(lambda m: main[:, i * GROUP + (GROUP + m)]))
            group(G_F, B_F, copy_to(lambda m: main[:, m]))

            for g in range(FG):
                act.wait_ge(mixer_done, g + 1)
                nc.scalar.copy(mixer[:, g], ps[:, 4 + g, 0:2 * P]).then_inc(mixer_ready, 1)
            for g in range(FG + 2):
                if g < FG:
                    act.wait_ge(ft_done, g + 1)
                    if g >= 2:
                        act.wait_ge(bank_done, B_FFT * GROUP + g - 1)
                    pair = 2 * (g % 2) + 4
                    nc.scalar.copy(half_ft[:, g % 2].rearrange("p t n -> p (t n)"),
                                   ps_flat[:, pair * 512:(pair + 2) * 512]).then_inc(ft_ready, 1)
                if g >= 2:
                    act.wait_ge(bank_done, B_FFT * GROUP + g - 1)
                    nc.scalar.copy(main[:, g - 2], ps[:, g - 2]).then_inc(bank_free, 1)
            act.dma_start(ident[:], ident_in).then_inc(attn_landed, 16)
            act.dma_start(identb[:], identb_in).then_inc(attn_landed, 16)
            act.dma_start(masks[:], masks_in).then_inc(attn_landed, 16)

            def tanh_bank(b, ready, m):
                act.wait_ge(bank_done, b * GROUP + (m + 1))
                act.wait_ge(tile_ready, ready + (m - 1))
                nc.scalar.activation(tmp[:, m % 2, 0:SEQ], ps[:, m], ACT.Tanh, scale=0.5).then_inc(tanh_done, 1)

            def residual_squares(b, index, t0):
                for m in range(GROUP):
                    act.wait_ge(bank_free, b * GROUP + (m + 1))
                    act.wait_ge(sq_added, index + (m - 1))
                    nc.scalar.activation(tmp[:, m % 2, 0:SEQ], main[:, t0 + m], ACT.Square).then_inc(squared, 1)

            with act.Fori(0, KV_HEADS) as i:
                for k in range(STEPS + 2):
                    if k in UNIT_SLOTS:
                        hi(i + G_Z, UNIT_SLOTS.index(k) + 2)
                    if k < STEPS:
                        width = score_width(k)
                        act.wait_ge(negmax_ready, i * STEPS + (k + 1))
                        nc.scalar.activation(probs[:, k % 2, 0:width], ps_flat[:, S_END - width:S_END], ACT.Exp,
                                             bias=stat[:, 1, k % 2:k % 2 + 1], scale=SCALE,
                                             accum_out=stat[:, 2, k % 2:k % 2 + 1]).then_inc(exp_done, 1)
                    if 1 <= k <= STEPS:
                        cols = score_width(k - 1) - 1
                        act.wait_ge(turned, i * STEPS + k)
                        nc.scalar.copy(probs_t[:, 0:cols], ps_flat[:, 6 * 512:6 * 512 + cols]).then_inc(probs_t_ready, 1)
                for m in range(GROUP):
                    tanh_bank(i + B_Z, i * GROUP + H_MIX0, m)
                hi(i + G_Z, HALVES + 1)

            for t in range(KT):
                split(H_MIX0 + t, main[:, t], h_hi[:, t])
            with act.Fori(0, 4) as i:
                for s in range(HALVES - 1):
                    hi(i + G_O, s + 2)
                residual_squares(i + B_O, i * GROUP + SQ_0, i * GROUP)
                hi(i + G_O, HALVES + 1)

            root(3, rstd[:])
            for t in range(KT):
                split(H_L1 + t, tmp[:, t % 2, 0:SEQ], h_hi[:, t], modv[:, 1, t:t + 1])
            with act.Fori(0, 4) as i:
                for s in range(HALVES - 1):
                    hi(i + G_U, s + 2)
                for m in range(GROUP):
                    act.wait_ge(bank_done, i * GROUP + (B_U * GROUP + m + 1))
                    act.wait_ge(ubuf_free, i * GROUP + (m + 1))
                    nc.scalar.copy(ubuf[:, m, PAD:PAD + SEQ], ps[:, m]).then_inc(bank_free, 1)
                hi(i + G_U, HALVES + 1)

            def pooled_hi(g, kt):
                act.wait_ge(ubuf_free, GROUP * (g + 1) + kt + 1)
                if g:
                    act.wait_ge(p_used, GROUP * (g - 1) + kt + 1)
                nc.scalar.copy(p_hi[:, kt], pooled[:, GROUP * g + kt]).then_inc(p_hi_ready, 1)

            for kt in range(GROUP):
                pooled_hi(0, kt)
            for g in range(GROUP):
                for half in range(2):
                    hi(G_GRP, 2 * g + half + 2, grp=None)
                    if g + 1 < GROUP:
                        pooled_hi(g + 1, 2 * half)
                        pooled_hi(g + 1, 2 * half + 1)
                for m in range(GROUP):
                    t = GROUP * g + m
                    act.wait_ge(p_used, GROUP * (g + 1))
                    nc.scalar.activation(pooled[:, t], ps[:, 4 * (g % 2) + m], ACT.Identity,
                                         scale=vec[:, V_LS + t:V_LS + t + 1]).then_inc(grp_free, 1)

            with act.Fori(0, 4) as i:
                for s in range(HALVES - 1):
                    hi(i + G_Z1, s + 2, grp=1)
                for m in range(GROUP):
                    tanh_bank(i + B_Z1, i * GROUP + H_MIX1, m)
                hi(i + G_Z1, HALVES + 1)
            for t in range(KT):
                split(H_MIX1 + t, pooled[:, t], h_hi[:, t])
            with act.Fori(0, 3) as i:
                for s in range(HALVES - 1):
                    hi(i + G_O1, s + 2, grp=1)
                residual_squares(i + B_O1, i * GROUP + SQ_1, i * GROUP)
                hi(i + G_O1, HALVES + 1)
            for s in range(HALVES - 2):
                hi(G_END - 1, s + 2, grp=1)
            residual_squares(B_O1 + 3, SQ_1 + 3 * GROUP, 3 * GROUP)
            root(4, rstd[:])

        @block.vector
        def _(dve):
            chain = Chain(dve, own)
            modv_flat = modv[:].rearrange("p a t -> p (a t)")

            def lo(n, j):
                dve.wait_ge(hi_ready, n * HALVES + (j + 1))
                nc.vector.tensor_tensor(w_lo[:, j % 2], raw[:, j % RAW_SLOTS], w_hi[:, j % 2].bitcast(F32),
                                        ALU.subtract).then_inc(lo_ready, 1)

            def job(cg, s):
                dve.wait_ge(chunk_landed[s % 2], (cg * GROUP + (s // 2 + 1)) * 16)
                for r in range(2):
                    kt = 2 * s + r
                    if kt:
                        dve.wait_ge(acc_step, cg * KT + kt)
                        ins = nc.vector.scalar_tensor_tensor(out=modacc[:], in0=modchunk[:, s % 2, r],
                                                             scalar=cond[:, kt, 0:1], in1=modacc[:],
                                                             op0=ALU.mult, op1=ALU.add)
                    else:
                        ins = nc.vector.tensor_scalar(modacc[:], modchunk[:, s % 2, r], cond[:, 0, 0:1], None,
                                                      ALU.mult)
                    ins.then_inc(acc_step, 1)

            def reduced(cg):
                dve.wait_ge(acc_reduced, cg + 1)
                nc.vector.tensor_tensor(modv_flat[:, bass.ds(cg * GROUP, GROUP)],
                                        ps[:, RED_BANK, RED_COL:RED_COL + GROUP],
                                        vec[:, bass.ds(cg * GROUP + V_BMB, GROUP)], ALU.add).then_inc(red_free, 1)

            def group(n, cg, finish, last=False):
                for s in range(HALVES - 1 if not last else HALVES - 2):
                    lo(n, s + 2)
                    if cg is not None:
                        if s == 0 and not (isinstance(cg, int) and cg == 0):
                            reduced(cg - 1)
                        job(cg, s)
                finish()
                if cg is not None:
                    job(cg, HALVES - 1)
                if not last:
                    lo(n, HALVES + 1)

            def add_square(index, dst, n, first):
                dve.wait_ge(squared, index + 1)
                t = tmp[:, index % 2, 0:n]
                if first:
                    nc.vector.tensor_copy(dst, t).then_inc(sq_added, 1)
                else:
                    dve.wait_ge(sq_added, index)
                    nc.vector.tensor_tensor(dst, dst, t, ALU.add).then_inc(sq_added, 1)

            def variance(k, sums, dst, n):
                dve.wait_ge(ssum_done, k)
                if k > 1:
                    dve.wait_ge(var_ready, k - 1)
                chain.link(nc.vector.tensor_scalar(scratch[:, 0:n], sums, 1.0 / D, EPS, ALU.mult, ALU.add))
                nc.vector.reciprocal(dst, scratch[:, 0:n]).then_inc(var_ready, 1)

            def normed(x, dst, g, r):
                nc.vector.scalar_tensor_tensor(out=dst, in0=x, scalar=g, in1=r, op0=ALU.mult,
                                               op1=ALU.mult).then_inc(tile_ready, 1)

            def split(index, x, hi_part, dst, shift=None):
                dve.wait_ge(split_hi, index + 1)
                h = hi_part.bitcast(F32)
                if shift is None:
                    ins = nc.vector.tensor_tensor(dst, x, h, ALU.subtract)
                else:
                    ins = nc.vector.scalar_tensor_tensor(out=dst, in0=x, scalar=shift, in1=h, op0=ALU.add,
                                                         op1=ALU.subtract)
                ins.then_inc(split_done, 1)

            def rotate(index, x):
                if not (isinstance(index, int) and index == 0):
                    dve.wait_ge(roped, index)
                for p in range(0, P, 32):
                    q = p ^ 32
                    nc.vector.tensor_tensor(scratch[q:q + 32, :], x[p:p + 32], rope[p:p + 32, 1], ALU.mult)
                chain.link(nc.vector.tensor_tensor(tmp[:, 0, 0:SEQ], x, rope[:, 0], ALU.mult))
                nc.vector.tensor_tensor(x, tmp[:, 0, 0:SEQ], scratch[:], ALU.add).then_inc(roped, 1)

            def residual(b, index, t0, layer_gate, ssum):
                for m in range(GROUP):
                    dve.wait_ge(bank_done, b * GROUP + (m + 1))
                    t = bass.ds(t0 + m, 1)
                    nc.vector.scalar_tensor_tensor(out=main[:, t0 + m], in0=ps[:, m], scalar=modv[:, layer_gate, t],
                                                   in1=main[:, t0 + m], op0=ALU.mult,
                                                   op1=ALU.add).then_inc(bank_free, 1)
                for m in range(GROUP):
                    dve.wait_ge(squared, index + (m + 1))
                    dve.wait_ge(sq_added, index + m)
                    nc.vector.tensor_tensor(ssum, ssum, tmp[:, m % 2, 0:SEQ], ALU.add).then_inc(sq_added, 1)

            def gate_mix(b, done, t0, buf):
                for m in range(GROUP):
                    dve.wait_ge(tanh_done, done + (m + 1))
                    t = tmp[:, m % 2, 0:SEQ]
                    nc.vector.scalar_tensor_tensor(out=t, in0=t, scalar=1.0, in1=ps[:, m], op0=ALU.add,
                                                   op1=ALU.mult).then_inc(bank_free, 1)
                    dve.wait_ge(bank_free, b * GROUP + (m + 1))
                    nc.vector.scalar_tensor_tensor(out=buf[:, t0 + m], in0=buf[:, t0 + m], scalar=0.5, in1=t,
                                                   op0=ALU.mult, op1=ALU.mult).then_inc(tile_ready, 1)

            nc.vector.memset(ones[:], 1.0).then_inc(ones_ready, 1)
            dve.wait_ge(cond_tanh, 1)
            c_in = vec[:, V_C:V_BM0].rearrange("p (t v) -> p t v", v=2)
            chain.link(nc.vector.scalar_tensor_tensor(out=cond[:], in0=cond_t[:], scalar=1.0, in1=c_in,
                                                      op0=ALU.add, op1=ALU.mult))
            nc.vector.tensor_scalar(cond[:], cond[:], 0.5, None, ALU.mult).then_inc(cond_ready, 1)
            sinks = vec[:, V_SINK:V_END]
            chain.link(nc.vector.tensor_scalar(sinks, sinks, 1.0 / SCALE, None, ALU.mult))

            for t in range(KT):
                add_square(SQ_X + t, ssq_x, SEQ, t == 0)
            for t in range(KT):
                add_square(SQ_C + t, ssq_c, CTX, t == 0)
            variance(1, ps[:, 5], rstd_x, SEQ)
            variance(2, ps[:, 6, 0:CTX], rstd_c, CTX)

            dve.wait_ge(mod0_done, 1)
            chain.link(nc.vector.tensor_tensor(mod0_v[:].rearrange("p a t v -> p (a t v)"),
                                               ps[:, MOD_BANK, 0:4 * KT], vec[:, V_BM0:V_BMB], ALU.add))
            for v in range(2):
                ins = nc.vector.scalar_tensor_tensor(out=gain[:, v], in0=mod0_v[:, 1, :, v], scalar=1.0,
                                                     in1=vec[:, V_G0:V_G1], op0=ALU.add, op1=ALU.mult)
            chain.link(ins)
            dve.wait_ge(rstd_ready, 2)

            def normed_pair(t):
                normed(main[:, t], main[:, t], gain[:, 0, t:t + 1], rstd_x)
                normed(ctx_t[:, t], ctx_t[:, t], gain[:, 1, t:t + 1], rstd_c)

            normed_pair(0)
            for t in range(KT):
                if t + 1 < KT:
                    normed_pair(t + 1)
                split(H_X + 2 * t, main[:, t], h_hi[:, t], h_lo[:, t], mod0_v[:, 0, t, 0:1])
                split(H_X + 2 * t + 1, ctx_t[:, t], hc_hi[:, t], hc_lo[:, t], mod0_v[:, 0, t, 1:2])
                if t in (1, 3):
                    lo(0, t // 2)

            def finish_keys():
                for m in range(GROUP):
                    dve.wait_ge(cbank_done, m + 1)
                    nc.vector.tensor_copy(keys_c[:, m], ps[:, 4 + m, 0:CTX]).then_inc(cbank_free, 1)
                dve.wait_ge(rope_landed, 32)
                for m in range(GROUP):
                    dve.wait_ge(bank_free, B_K * GROUP + m + 1)
                    rotate(m, keys[:, m])

            def finish_values():
                for m in range(CTX_TILES):
                    dve.wait_ge(cbank_done, GROUP + m + 1)
                    nc.vector.tensor_copy(values_c[:, m], ps[:, 4 + m]).then_inc(cbank_free, 1)

            group(G_K, M_K, finish_keys)
            group(G_V, M_V, finish_values)
            per = GROUP
            with dve.Fori(0, 3) as i:
                chain.loop(i, per)

                def finish_queries():
                    for m in range(GROUP):
                        dve.wait_ge(bank_free, i * GROUP + (B_Q * GROUP + m + 1))
                        rotate(i * GROUP + (GROUP + m), main[:, i * GROUP + (GROUP + m)])

                group(i + G_Q, i + M_Q, finish_queries)
            chain.end(3)
            group(G_F, M_F, lambda: None)
            reduced(M_FFT - 1)
            for s in range(HALVES):
                job(M_FFT, s)

            dve.wait_ge(bank_done, (B_FFT + 1) * GROUP)
            dve.wait_ge(roped, 16)
            dve.wait_ge(bank_free, (B_V + 1) * GROUP)
            dve.wait_ge(cbank_free, GROUP + CTX_TILES)
            with dve.Fori(0, KV_HEADS) as i:
                chain.loop(i, 2 * STEPS)
                nc.vector.tensor_copy(q_cur[:], main[:, bass.ds(i * GQA + FG, GQA)])
                nc.vector.tensor_copy(v_cur[:, 0:BLOCKS], values[:, :, bass.ds(i * P, P)])
                nc.vector.tensor_copy(v_cur[:, BLOCKS:], values_c[:, :, bass.ds(i * P, P)]).then_inc(qv_ready, 1)
                for k in range(STEPS + 2):
                    par = k % 2
                    if k < STEPS:
                        width = score_width(k)
                        dve.wait_ge(scores_done, i * STEPS + (k + 1))
                        chain.link(nc.vector.tensor_reduce(stat[:, 0, par:par + 1], ps_flat[:, S_END - width:S_END],
                                                           AX.X, ALU.max))
                        nc.vector.tensor_scalar(stat[:, 1, par:par + 1], stat[:, 0, par:par + 1], -SCALE, None,
                                                ALU.mult).then_inc(negmax_ready, 1)
                    if k == 0:
                        reduced(i + (M_Z - 1))
                    if k in UNIT_SLOTS:
                        lo(i + G_Z, UNIT_SLOTS.index(k) + 2)
                    if k >= 2:
                        n, j = divmod(k - 2, GQA)
                        dve.wait_ge(pv_done, i * STEPS + (k - 1))
                        nc.vector.tensor_scalar(main[:, i * GQA + (FG + j), n * P:(n + 1) * P], ps[:, 7, P:2 * P],
                                                1.0, None, ALU.mult).then_inc(y_done, 1)
                    if k in JOB_SLOTS:
                        job(i + M_Z, JOB_SLOTS.index(k))
                    if k < STEPS:
                        dve.wait_ge(exp_done, i * STEPS + (k + 1))
                        chain.link(nc.vector.reciprocal(stat[:, 3, par:par + 1], stat[:, 2, par:par + 1]))
                        p = probs[:, par, 0:width - 1]
                        nc.vector.tensor_scalar(p, p, stat[:, 3, par:par + 1], None,
                                                ALU.mult).then_inc(probs_ready, 1)
                dve.wait_ge(y_done, i * STEPS + STEPS)
                gate_mix(i + B_Z, i * GROUP, i * GROUP, main)
                lo(i + G_Z, HALVES + 1)
            chain.end(KV_HEADS)

            chain.link(nc.vector.memset(ssum, 0.0))
            for t in range(KT):
                split(H_MIX0 + t, main[:, t], h_hi[:, t], h_lo[:, t])
            with dve.Fori(0, 4) as i:
                def finish_out():
                    dve.wait_ge(res_landed, 16 * 4)
                    residual(i + B_O, i * GROUP + SQ_0, i * GROUP, 0, ssum)

                group(i + G_O, i + M_O, finish_out)
            reduced(M_GRP - 1)
            dve.wait_ge(red_free, M_GRP)
            variance(3, ps[:, 5], rstd[:], SEQ)
            chain.link(nc.vector.scalar_tensor_tensor(out=gain[:, 2], in0=modv[:, 2], scalar=1.0,
                                                      in1=vec[:, V_G1:V_GF], op0=ALU.add, op1=ALU.mult))
            dve.wait_ge(rstd_ready, 3)
            normed(main[:, 0], tmp[:, 0, 0:SEQ], gain[:, 2, 0:1], rstd[:])
            for t in range(KT):
                if t + 1 < KT:
                    if t:
                        dve.wait_ge(split_done, H_L1 + t)
                    normed(main[:, t + 1], tmp[:, (t + 1) % 2, 0:SEQ], gain[:, 2, t + 1:t + 2], rstd[:])
                split(H_L1 + t, tmp[:, t % 2, 0:SEQ], h_hi[:, t], h_lo[:, t], modv[:, 1, t:t + 1])

            for m in range(GROUP):
                nc.vector.memset(ubuf[:, m], 0.0).then_inc(ubuf_free, 1)

            def pool_tile(g, m):
                w = POOL_WINDOWS[g]
                t = GROUP * g + m
                dve.wait_ge(bank_free, (B_U + g) * GROUP + m + 1)
                dve.wait_ge(ubuf_free, GROUP + t)
                src, size = ubuf[:, m], WIDE
                step, buf = 1, 0
                while step < w:
                    size -= step
                    chain.link(nc.vector.tensor_tensor(tmp[:, buf, 0:size], src[:, 0:size],
                                                       src[:, step:step + size], ALU.add))
                    src, step, buf = tmp[:, buf], 2 * step, 1 - buf
                win = src[:, PAD - w // 2:PAD - w // 2 + SEQ]
                ends = win.rearrange("p (a b) -> p a b", b=PAD)[:, 0:SEQ // PAD:SEQ // PAD - 1]
                chain.link(nc.vector.tensor_tensor(ends, ends, edges[:, g], ALU.mult))
                nc.vector.scalar_tensor_tensor(out=pooled[:, t], in0=win, scalar=1.0 / w, in1=ubuf[:, m, PAD:PAD + SEQ],
                                               op0=ALU.mult, op1=ALU.subtract).then_inc(ubuf_free, 1)

            for g in range(GROUP):
                group(G_U + g, None, lambda: [pool_tile(g, m) for m in range(GROUP)])

            def pooled_lo(g, kt):
                dve.wait_ge(p_hi_ready, GROUP * g + kt + 1)
                nc.vector.tensor_tensor(p_lo[:, kt], pooled[:, GROUP * g + kt], p_hi[:, kt].bitcast(F32),
                                        ALU.subtract).then_inc(p_ready, 1)

            for kt in range(GROUP):
                pooled_lo(0, kt)
            for g in range(GROUP):
                for half in range(2):
                    lo(G_GRP, 2 * g + half + 2)
                    if g + 1 < GROUP:
                        pooled_lo(g + 1, 2 * half)
                        pooled_lo(g + 1, 2 * half + 1)
                    job(M_GRP, 2 * g + half)

            def group_z1(i):
                group(i + G_Z1, None, lambda: gate_mix(i + B_Z1, (i + KV_HEADS) * GROUP, i * GROUP, pooled))

            with dve.Fori(0, 4) as i:
                group_z1(i)
            reduced(M_GRP)
            for t in range(KT):
                split(H_MIX1 + t, pooled[:, t], h_hi[:, t], h_lo[:, t])
            chain.link(nc.vector.memset(ssum, 0.0))
            dve.wait_ge(red_free, M_END)
            with dve.Fori(0, 3) as i:
                group(i + G_O1, None, lambda: residual(i + B_O1, i * GROUP + SQ_1, i * GROUP, 3, ssum))
            group(G_END - 1, None, lambda: residual(B_O1 + 3, SQ_1 + 3 * GROUP, 3 * GROUP, 3, ssum), last=True)
            variance(4, ps[:, 5], rstd[:], SEQ)
            dve.wait_ge(rstd_ready, 4)
            for t in range(KT):
                nc.vector.scalar_tensor_tensor(out=main[:, t], in0=main[:, t], scalar=vec[:, V_GF + t:V_GF + t + 1],
                                               in1=rstd[:], op0=ALU.mult, op1=ALU.mult).then_inc(out_ready, 1)

        @block.tensor
        def _(pe):
            def mm(out, lhsT, rhs, start, stop):
                return nc.tensor.matmul(out, lhsT, rhs, start=start, stop=stop, skip_group_check=True)

            def three(out, a_hi, a_lo, b_hi, b_lo, start, stop):
                mm(out, a_hi, b_hi, start, False)
                mm(out, a_hi, b_lo, False, False)
                return mm(out, a_lo, b_hi, False, stop)

            def unit_bank(s, m, x_hi=h_hi, x_lo=h_lo, n=SEQ, bank=0):
                for r in range(2):
                    kt, cols = 2 * s + r, slice(m * P, (m + 1) * P)
                    ins = three(ps[:, bank + m, 0:n], w_hi[:, s % 2, r, cols], w_lo[:, s % 2, r, cols],
                                x_hi[:, kt], x_lo[:, kt], kt == 0, kt == KT - 1)
                return ins

            def token_bank(s, m, x_hi=h_hi, x_lo=h_lo, bank=0):
                for r in range(2):
                    kt, toks = 2 * s + r, slice(m * P, (m + 1) * P)
                    ins = three(ps[:, bank + m], x_hi[:, kt, toks], x_lo[:, kt, toks],
                                w_hi[:, s % 2, r], w_lo[:, s % 2, r], kt == 0, kt == KT - 1)
                return ins

            def unit(n, b, s, m, make=unit_bank, signal=None):
                if m == 0:
                    pe.wait_ge(lo_ready, n * HALVES + (s + 1))
                if s == 0 and not (isinstance(b, int) and b == 0):
                    pe.wait_ge(bank_free, b * GROUP + (m + 1 - GROUP))
                ins = make(s, m)
                if s == HALVES - 1:
                    ins.then_inc(bank_done, 1)
                elif m == GROUP - 1:
                    ins.then_inc(weights_used, 1)

            def reduce(cg):
                pe.wait_ge(acc_step, cg * KT + KT)
                if not (isinstance(cg, int) and cg == 0):
                    pe.wait_ge(red_free, cg)
                for m in range(GROUP):
                    ins = mm(ps[:, RED_BANK, RED_COL + m:RED_COL + m + 1], modacc[:, m * P:(m + 1) * P], ones[:, 0:1],
                             m == 0, True)
                ins.then_inc(acc_reduced, 1)

            def group(n, b, split_base, cg=None, make=unit_bank):
                for s in range(HALVES):
                    if split_base is not None:
                        pe.wait_ge(split_done, split_base + 2 * s + 2)
                    for m in range(GROUP):
                        unit(n, b, s, m, make)
                    if s == 0 and cg is not None:
                        reduce(cg)

            def sum_squares(k, index, bank, sums, n):
                pe.wait_ge(sq_added, index)
                mm(ps[:, bank, 0:n], ones[:], sums, True, True).then_inc(ssum_done, 1)

            pe.wait_ge(ones_ready, 1)
            pe.wait_ge(cond_ready, 1)

            def mod0_group(cg):
                for s in range(HALVES):
                    pe.wait_ge(raw_landed[s % RAW_SLOTS], (cg * 2 + (s // RAW_SLOTS + 1)) * 16)
                    for r in range(2):
                        for m in range(GROUP):
                            kt = 2 * s + r
                            ins = mm(ps[:, MOD_BANK, bass.ds((cg * GROUP + m) * 2, 2)],
                                     raw[:, s % RAW_SLOTS, r, m * P:(m + 1) * P], cond[:, kt],
                                     kt == 0 and m == 0, kt == KT - 1)
                    ins.then_inc(mod0_used, 1)

            with pe.Fori(0, GROUP) as i:
                mod0_group(i)
            sum_squares(1, SQ_C, 5, ssq_x, SEQ)
            sum_squares(2, SQ_0, 6, ssq_c, CTX)
            with pe.Fori(GROUP, 2 * GROUP) as i:
                mod0_group(i)
            pe.wait_ge(mod0_used, MOD0_HALVES)
            pe.sem_inc(mod0_done, 1)

            for s in range(HALVES):
                pe.wait_ge(split_done, 4 * s + 4)
                for m in range(GROUP):
                    if m == 0:
                        pe.wait_ge(lo_ready, s + 1)
                    ins = unit_bank(s, m)
                    if s == HALVES - 1:
                        ins.then_inc(bank_done, 1)
                    ins = unit_bank(s, m, hc_hi, hc_lo, CTX, 4)
                    if s == HALVES - 1:
                        ins.then_inc(cbank_done, 1)
                    elif m == GROUP - 1:
                        ins.then_inc(weights_used, 1)

            pe.wait_ge(cbank_free, GROUP)
            for s in range(HALVES):
                pe.wait_ge(lo_ready, G_V * HALVES + s + 1)
                for m in range(GROUP):
                    if s == 0:
                        pe.wait_ge(bank_free, B_V * GROUP + m + 1 - GROUP)
                    ins = token_bank(s, m)
                    if s == HALVES - 1:
                        ins.then_inc(bank_done, 1)
                for m in range(CTX_TILES):
                    ins = token_bank(s, m, hc_hi, hc_lo, 4)
                    if s == HALVES - 1:
                        ins.then_inc(cbank_done, 1)
                if s < HALVES - 1:
                    ins.then_inc(weights_used, 1)
                if s == 0:
                    reduce(M_V - 1)
            with pe.Fori(0, 3) as i:
                group(i + G_Q, i + B_Q, None, i + (M_Q - 1))
            group(G_F, B_F, None, M_F - 1)

            pe.wait_ge(fft_landed, 48)
            pe.wait_ge(cbank_free, GROUP + CTX_TILES)
            pe.wait_ge(red_free, M_F)
            for g in range(FG):
                for c in range(2):
                    ins = mm(ps[:, 4 + g, c * P:(c + 1) * P], dft_ch[:, c], wf_sb[:, g], c == 0, True)
                ins.then_inc(mixer_done, 1)
            pe.wait_ge(mixer_ready, FG)
            reduce(M_FFT - 1)
            pe.wait_ge(bank_free, (B_F + 1) * GROUP)
            for g in range(FG + 1):
                if g < FG:
                    if g == 1:
                        pe.wait_ge(red_free, M_FFT)
                    if g >= 2:
                        pe.wait_ge(ft_ready, g - 1)
                    for t in range(BLOCKS):
                        ins = mm(ps[:, 4 + 2 * (g % 2) + t // 2, 256 * (t % 2):256 * (t % 2) + 256],
                                 main[:, g, t * P:(t + 1) * P], mixer[:, g], t % 2 == 0, True)
                    ins.then_inc(ft_done, 1)
                if g >= 1:
                    f = g - 1
                    pe.wait_ge(ft_ready, f + 1)
                    for c in range(2):
                        for t in range(BLOCKS):
                            ins = mm(ps[:, f], half_ft[:, f % 2, t, c * P:(c + 1) * P], dft_tok[:, c, t],
                                     c == 0 and t == 0, c == 1 and t == BLOCKS - 1)
                    ins.then_inc(bank_done, 1)

            pe.wait_ge(attn_landed, 48)

            def scores(i, k):
                n, j = divmod(k, GQA)
                first, end = block_tiles(n)
                if k:
                    pe.wait_ge(exp_done, i * STEPS + k)
                q = q_cur[:, j, n * P:(n + 1) * P]
                at = 512 - (end - first) * P
                mm(ps[:, 4, at:512], q, keys[:, i, first * P:end * P], True, False)
                if n > first:
                    mm(ps[:, 4, at:at + P], identb[:], masks[:, 0], False, False)
                if end > n + 1:
                    mm(ps[:, 4, 512 - P:512], identb[:], masks[:, 1], False, True)
                mm(ps[:, 5, 0:CTX], q, keys_c[:, i], True, True)
                mm(ps[:, 5, CTX:CTX + 1], ones[:], vec[:, bass.ds(i * GQA + (V_SINK + j), 1)], False,
                   True).then_inc(scores_done, 1)

            def turn(i, k):
                pe.wait_ge(probs_ready, i * STEPS + (k + 1))
                if k >= 1:
                    pe.wait_ge(y_done, i * STEPS + k)
                for t in range(score_width(k) // P):
                    ins = nc.tensor.transpose(ps_flat[:, 6 * 512 + t * P:6 * 512 + (t + 1) * P],
                                              probs[:, k % 2, t * P:(t + 1) * P], ident[:])
                ins.then_inc(turned, 1)

            def attend(i, k):
                first, end = block_tiles(k // GQA)
                tiles = list(range(first, end)) + [BLOCKS, BLOCKS + 1]
                pe.wait_ge(probs_t_ready, i * STEPS + (k + 1))
                if k == 0:
                    pe.wait_ge(red_free, i + M_Z)
                for c, t in enumerate(tiles):
                    ins = mm(ps[:, 7, P:2 * P], v_cur[:, t], probs_t[:, c * P:(c + 1) * P], c == 0,
                             c == len(tiles) - 1)
                ins.then_inc(pv_done, 1)

            with pe.Fori(0, KV_HEADS) as i:
                step = 0
                for k, count in enumerate(BANK_STEPS):
                    if k >= 2:
                        attend(i, k - 2)
                    if 0 < k < STEPS:
                        scores(i, k)
                    if 0 < k <= STEPS:
                        turn(i, k - 1)
                    for _ in range(count):
                        unit(i + G_Z, i + B_Z, *divmod(step, GROUP))
                        step += 1
                    if k == 0:
                        pe.wait_ge(qv_ready, i + 1)
                        scores(i, 0)
                        reduce(i + (M_Z - 1))
                pe.wait_ge(y_done, i * STEPS + STEPS)

            with pe.Fori(0, 4) as i:
                group(i + G_O, i + B_O, H_MIX0, i + (M_O - 1))
            reduce(M_GRP - 1)
            sum_squares(3, SQ_1, 5, ssum, SEQ)
            with pe.Fori(0, 4) as i:
                group(i + G_U, i + B_U, H_L1)

            pe.wait_ge(red_free, M_GRP)
            for g in range(GROUP):
                for kt in range(GROUP):
                    s = 2 * g + kt // 2
                    pe.wait_ge(p_ready, GROUP * g + kt + 1)
                    pe.wait_ge(lo_ready, G_GRP * HALVES + s + 1)
                    for m in range(GROUP):
                        if kt == 0 and g < 2:
                            pe.wait_ge(bank_free, B_Z1 * GROUP + m + 1 - GROUP)
                        if kt == 0 and g >= 2:
                            pe.wait_ge(grp_free, GROUP * (g - 2) + m + 1)
                        cols = slice(m * P, (m + 1) * P)
                        ins = three(ps[:, 4 * (g % 2) + m], w_hi[:, s % 2, kt % 2, cols], w_lo[:, s % 2, kt % 2, cols],
                                    p_hi[:, kt], p_lo[:, kt], kt == 0, kt == GROUP - 1)
                    ins.then_inc(p_used, 1)
            pe.wait_ge(grp_free, GROUP * GROUP)
            reduce(M_GRP)

            with pe.Fori(0, 4) as i:
                group(i + G_Z1, i + B_Z1, None)
            with pe.Fori(0, 4) as i:
                group(i + G_O1, i + B_O1, H_MIX1)
            sum_squares(4, 4 * KT, 5, ssum, SEQ)


def stream(w, col_groups):
    parts = [w[:, g * COLS:(g + 1) * COLS].reshape(-1, 2, P, COLS).transpose(0, 2, 1, 3).reshape(-1, P, 2 * COLS)
             for g in col_groups]
    return np.concatenate(parts)


def per_partition(v):
    return v.reshape(-1, P).T


def rope_tables():
    pairs = P // 4
    inv = 1.0 / 10000.0 ** (np.arange(pairs) / pairs)
    tok = np.arange(SEQ)
    angle = np.concatenate([np.outer(inv, pos) for pos in (tok // 64, tok // 64, tok % 64, tok % 64)])
    sign = np.repeat([1.0, -1.0, 1.0, -1.0], pairs)[:, None]
    return np.stack([np.cos(angle), sign * np.sin(angle)], axis=1).astype(np.float32)


def constants():
    bf16 = mybir.dt.np(BF16)
    q = np.arange(P)[:, None]
    k = np.arange(P)[None, :]
    masks = np.stack([np.where(k >= q, 0.0, MASKED), np.where(k <= q, 0.0, MASKED)], axis=1)
    tok = 2 * np.pi / SEQ * (np.outer(np.arange(SEQ), np.arange(SEQ)) % SEQ)
    norm = 1.0 / np.sqrt(SEQ * P)
    dft_tok = np.stack([np.cos(tok) * norm, -np.sin(tok) * norm]).reshape(2, BLOCKS, P, SEQ).transpose(2, 0, 1, 3)
    ch = 2 * np.pi / P * (np.outer(np.arange(P), np.arange(P)) % P)
    dft_ch = np.stack([np.cos(ch), np.sin(ch)], axis=1)
    edges = np.ones((GROUP, 2, PAD))
    for g, w in enumerate(POOL_WINDOWS):
        for e, first in enumerate((0, SEQ - PAD)):
            for c in range(PAD):
                t = first + c
                edges[g, e, c] = w / (min(t - w // 2 + w, SEQ) - max(t - w // 2, 0))
    f32 = np.float32
    return {
        "ident": np.eye(P, dtype=f32), "identb": np.eye(P).astype(bf16),
        "masks": masks.astype(bf16), "rope": rope_tables(), "dft_tok": dft_tok.astype(f32),
        "dft_ch": dft_ch.astype(f32), "edges": np.broadcast_to(edges, (P,) + edges.shape).astype(f32),
    }


def layouts(x, c, ctx, c_ctx, l0_norm, l0_w_mod, l0_b_mod, l0_w_in, l0_sink, l0_w_f, l0_w_out,
            l1_norm, l1_w_mod, l1_b_mod, l1_w_in, l1_w_grp, l1_scale, l1_w_out, final_norm):
    mixed = np.roll(np.arange(KT), FG)
    q0, k0, v0, f0, z0 = 0, 3, 4, 5, 6
    in0 = stream(l0_w_in, [k0, v0, q0, q0 + 1, q0 + 2, f0, z0 + 3, z0, z0 + 1, z0 + 2])
    out0 = stream(l0_w_out.reshape(KT, P, D)[mixed].reshape(D, D), range(4))
    in1 = stream(l1_w_in, range(4))
    grp = np.concatenate([stream(l1_w_grp[g], [0]) for g in range(GROUP)])
    gate1 = stream(l1_w_in, range(4, 8))
    out1 = stream(l1_w_out, range(4))
    cond = np.stack([per_partition(c[0]), per_partition(c_ctx)], axis=2).reshape(P, -1)
    b0 = per_partition(l0_b_mod)
    sink = np.zeros((P, HEADS), np.float32)
    sink[0] = l0_sink
    vectors = np.concatenate([
        cond, np.repeat(b0[:, 0:2 * KT], 2, axis=1), b0[:, 2 * KT:], per_partition(l1_b_mod),
        per_partition(l0_norm), per_partition(l1_norm), per_partition(final_norm), per_partition(l1_scale), sink,
    ], axis=1)
    return {
        "mod0": stream(l0_w_mod, range(8)),
        "weights": np.concatenate([in0, out0, in1, grp, gate1, out1]),
        "modb": np.concatenate([stream(l0_w_mod, range(8, 12)), stream(l1_w_mod, range(12))]),
        "xT": x[0].T.reshape(KT, P, SEQ), "ctxT": ctx[0].T.reshape(KT, P, CTX),
        "vectors": vectors, "wf": l0_w_f,
    }


def kernel(**inputs):
    import concourse.bacc as bacc
    from concourse.bass_utils import run_bass_kernel_spmd

    nc = bacc.Bacc("TRN2", target_bir_lowering=False, num_devices=1)
    arrays, args = {}, []
    for name, a in {**layouts(**{k: np.asarray(v) for k, v in inputs.items()}), **constants()}.items():
        arrays[f"in_{name}"] = np.ascontiguousarray(a)
        args.append(nc.dram_tensor(f"in_{name}", a.shape, mybir.dt.from_np(a.dtype), kind="ExternalInput").ap())
    out = nc.dram_tensor("out", (KT, P, SEQ), F32, kind="ExternalOutput").ap()
    build(nc, *args, out)
    result = run_bass_kernel_spmd(nc, [arrays], core_ids=[0]).results[0]["out"]
    return np.ascontiguousarray(np.asarray(result).reshape(D, SEQ).T)[None]
```

```python
from contextlib import ExitStack

import numpy as np

import concourse.bass as bass
from concourse import mybir

P = 128
D = 2048
SEQ = 512
CTX = 256
KT = D // P
GROUP = 4
COLS = GROUP * P
HALVES = KT // 2
HEADS, KV_HEADS = 12, 4
GQA = HEADS // KV_HEADS
BLOCKS = SEQ // P
CTX_TILES = CTX // P
STEPS = BLOCKS * GQA
FG = 4
POOL_WINDOWS = (2, 4, 8, 16)
PAD = 8
WIDE = SEQ + 2 * PAD
SCALE = float(P) ** -0.5
EPS = 1e-6
MASKED = -1.0e30
RAW_SLOTS = 4


def starts(*sizes):
    return np.cumsum((0,) + sizes).tolist()


G_M, G_K, G_V, G_Q, G_F, G_Z, G_O, G_U, G_GRP, G_Z1, G_O1, G_END = starts(8, 1, 1, 3, 1, 4, 4, 4, 1, 4, 4)
B_K, B_V, B_Q, B_F, B_FFT, B_Z, B_O, B_U, B_Z1, B_O1 = starts(1, 1, 3, 1, 1, 4, 4, 4, 4)
M_K, M_V, M_Q, M_F, M_FFT, M_Z, M_O, M_GRP, M_END = starts(1, 1, 3, 1, 1, 4, 4, 1)
H_X, H_MIX0, H_L1, H_MIX1 = starts(2 * KT, KT, KT)
SQ_X, SQ_C, SQ_0, SQ_1 = starts(KT, KT, KT)
SUM_0, SUM_1, SUM_END = starts(2 + KT, 2 + KT)
PIECES, PIECES_BEFORE = 8, 3
V_C, V_BM0, V_BMB, V_G0, V_G1, V_GF, V_LS, V_SINK, V_ID, V_END = starts(
    2 * KT, 4 * KT, 4 * KT, KT, KT, KT, KT, HEADS, 4)

ALU = mybir.AluOpType
ACT = mybir.ActivationFunctionType
AX = mybir.AxisListType
F32 = mybir.dt.float32
F32R = mybir.dt.float32r
BF16 = mybir.dt.bfloat16


class Chain:

    def __init__(self, eng, sem):
        self.eng, self.sem, self.base, self.n = eng, sem, 0, 0

    def link(self, ins):
        self.n += 1
        ins.then_inc(self.sem, 1)
        self.eng.wait_ge(self.sem, self.base + self.n)

    def loop(self, i, per):
        self.before, self.per = self.n, per
        self.base = i * per

    def end(self, trips):
        assert self.n == self.before + self.per, (self.n - self.before, self.per)
        self.base, self.n = 0, self.before + self.per * trips


def block_tiles(n):
    return max(n - 1, 0), min(n + 2, BLOCKS)


def score_width(k):
    first, end = block_tiles(k // GQA)
    return (end - first) * P + CTX + 1


UNIT_SLOTS = (2, 4, 6, 8, 10, 12, 13)
QUERY_SLOTS = (1, 4, 7)
JOB_SLOTS = (1, 3, 5, 7, 9, 11, 12, 13)
BANK_STEPS = (2,) * STEPS + (4, 4)


def build(nc, weights, modb, xT, ctxT, vectors, wf, ident_in, identb_in, masks_in, rope_in, dft_tok_in,
          dft_ch_in, edges_in, outT):
    with ExitStack() as whole:
        def sb(name, shape, dt, scope=whole):
            return scope.enter_context(nc.sbuf_tensor(name, shape, dt))

        def sem(name):
            return whole.enter_context(nc.semaphore(name))

        raw = sb("raw", [P, RAW_SLOTS, 2, COLS], F32)
        w_hi = sb("w_hi", [P, 2, 2, COLS], F32R)
        w_lo = sb("w_lo", [P, 2, 2, COLS], F32R)
        h_hi = sb("h_hi", [P, KT, SEQ], F32R)
        h_lo = sb("h_lo", [P, KT, SEQ], F32R)
        main = sb("main", [P, KT, SEQ], F32)
        tmp = sb("tmp", [P, 2, WIDE], F32)
        scratch = sb("scratch", [P, SEQ], F32)
        vec = sb("vec", [P, V_END], F32)
        ones_r = sb("ones_r", [P, P], F32R)
        ones = ones_r[:].bitcast(F32)
        sink_hi = sb("sink_hi", [P, HEADS, 2], F32R)
        sink_lo = sb("sink_lo", [P, HEADS, 2], F32R)
        cond = sb("cond", [P, KT, 2], F32)
        cond_split = sb("cond_split", [P, KT, 2, 2], F32R)
        cond_t = sb("cond_t", [P, KT, 2], F32)
        mod0_v = sb("mod0_v", [P, 2, KT, 2], F32)
        modv = sb("modv", [P, 4, KT], F32)
        gain = sb("gain", [P, 3, KT], F32)
        edges = sb("edges", [P, GROUP, 2, PAD], F32)
        stat = sb("stat", [P, 4, 2], F32)
        modchunk = sb("modchunk", [P, 2, 2, COLS], F32)
        modacc = sb("modacc", [P, COLS], F32)

        kv_cols = 2 * (SEQ + CTX) * KV_HEADS + 2 * SEQ
        with ExitStack() as s:
            kvmem = sb("kvmem", [P, kv_cols], F32, s)
            with ExitStack() as z:
                hc_hi = sb("hc_hi", [P, KT, CTX], F32R, z)
                hc_lo = sb("hc_lo", [P, KT, CTX], F32R, z)
            with ExitStack() as z:
                dft_tok = sb("dft_tok", [P, 2, BLOCKS, SEQ], F32, z)
                dft_ch = sb("dft_ch", [P, 2, P], F32, z)
                wf_sb = sb("wf_sb", [P, FG, P], F32, z)
                mixer = sb("mixer", [P, FG, 2 * P], F32, z)
                half_ft = sb("half_ft", [P, 2, BLOCKS, 2 * P], F32, z)
            with ExitStack() as z:
                probs = sb("probs", [P, 2, 5 * P + 1], F32, z)
                pt_hi = sb("pt_hi", [P, 5 * P], F32R, z)
                pt_lo = sb("pt_lo", [P, 5 * P], F32R, z)
                q_hi = sb("q_hi", [P, 2, GQA, P], F32R, z)
                q_lo = sb("q_lo", [P, 2, GQA, P], F32R, z)
                k_hi = sb("k_hi", [P, SEQ + CTX], F32R, z)
                k_lo = sb("k_lo", [P, SEQ + CTX], F32R, z)
                v_hi = sb("v_hi", [P, BLOCKS + CTX_TILES, P], F32R, z)
                v_lo = sb("v_lo", [P, BLOCKS + CTX_TILES, P], F32R, z)
                ident = sb("ident", [P, P], F32, z)
                identb = sb("identb", [P, P], BF16, z)
                masks = sb("masks", [P, 2, P], BF16, z)
            with ExitStack() as z:
                pooled = sb("pooled", [P, KT, SEQ], F32, z)
        with ExitStack() as s:
            p_hi = sb("p_hi", [P, GROUP, SEQ], F32R, s)
            p_lo = sb("p_lo", [P, GROUP, SEQ], F32R, s)
            ubuf = sb("ubuf", [P, GROUP, WIDE], F32, s)
            rstd = sb("rstd", [P, SEQ], F32, s)

        def kv_part(at, shape):
            n = int(np.prod(shape))
            view = kvmem[:, at:at + n]
            return view if len(shape) == 1 else view.rearrange("p (a b) -> p a b", a=shape[0])

        k_keys, k_values, k_kc, k_vc, k_rope, _ = starts(*[n * KV_HEADS for n in (SEQ, SEQ, CTX, CTX)], 2 * SEQ)
        keys = kv_part(k_keys, [KV_HEADS, SEQ])
        values = kv_part(k_values, [BLOCKS, KV_HEADS * P])
        keys_c = kv_part(k_kc, [KV_HEADS, CTX])
        values_c = kv_part(k_vc, [CTX_TILES, KV_HEADS * P])
        rope = kv_part(k_rope, [2, SEQ])
        ctx_t = kv_part(k_keys, [KT, CTX])
        rstd_x = kv_part(k_kc, [SEQ])
        rstd_c = kv_part(k_kc + SEQ, [CTX])
        mod_hi = [w_hi[:, 0], w_hi[:, 1], h_hi[:, 0:2], h_hi[:, 2:4]]
        mod_lo = [w_lo[:, 0], w_lo[:, 1], h_lo[:, 0:2], h_lo[:, 2:4]]
        mod_rows = kvmem[0:4, k_vc:k_vc + COLS]
        ssum = ubuf[:, 0, 0:SEQ]

        ps = whole.enter_context(nc.psum_tensor("ps", [P, 8, 512], F32))
        ps_flat = ps[:].rearrange("p b n -> p (b n)")
        MOD_BANK, RED_BANK, RED_COL = 4, 7, 384
        S_END = 6 * 512 - 256 + 1

        raw_landed = [sem(f"raw_landed{i}") for i in range(RAW_SLOTS)]
        chunk_landed = [sem(f"chunk_landed{i}") for i in range(2)]
        x_landed = sem("x_landed")
        res_landed = sem("res_landed")
        ctx_landed, vec_landed, rope_landed = sem("ctx_landed"), sem("vec_landed"), sem("rope_landed")
        fft_landed, attn_landed, stored = sem("fft_landed"), sem("attn_landed"), sem("stored")
        ones_ready, own = sem("ones_ready"), sem("own")
        cond_tanh, cond_ready = sem("cond_tanh"), sem("cond_ready")
        cond_hi_ready, cond_split_ready = sem("cond_hi_ready"), sem("cond_split_ready")
        sinks_ready, sinks_hi_ready = sem("sinks_ready"), sem("sinks_hi_ready")
        rows_done, rows_ready, rows_turned = sem("rows_done"), sem("rows_ready"), sem("rows_turned")
        acc_step, acc_reduced, red_free = sem("acc_step"), sem("acc_reduced"), sem("red_free")
        squared, sq_summed, sq_added = sem("squared"), sem("sq_summed"), sem("sq_added")
        ssum_done, var_ready, rstd_ready = sem("ssum_done"), sem("var_ready"), sem("rstd_ready")
        hi_ready, lo_ready, weights_used = sem("hi_ready"), sem("lo_ready"), sem("weights_used")
        tile_ready, split_hi, split_done = sem("tile_ready"), sem("split_hi"), sem("split_done")
        bank_done, bank_free = sem("bank_done"), sem("bank_free")
        cbank_done, cbank_free = sem("cbank_done"), sem("cbank_free")
        roped = sem("roped")
        mixer_done, mixer_ready = sem("mixer_done"), sem("mixer_ready")
        ft_done, ft_ready = sem("ft_done"), sem("ft_ready")
        swapped, swap_begun, piece_hi, piece_ready = sem("swapped"), sem("swap_begun"), sem("piece_hi"), sem("piece_ready")
        scores_done, negmax_ready = sem("scores_done"), sem("negmax_ready")
        exp_done, probs_ready, turned = sem("exp_done"), sem("probs_ready"), sem("turned")
        pt_hi_ready, pt_ready, pv_done, y_done = sem("pt_hi_ready"), sem("pt_ready"), sem("pv_done"), sem("y_done")
        tanh_done = sem("tanh_done")
        ubuf_free = sem("ubuf_free")
        p_hi_ready, p_ready, p_used = sem("p_hi_ready"), sem("p_ready"), sem("p_used")
        grp_free = sem("grp_free")
        out_ready = sem("out_ready")

        block = whole.enter_context(nc.Block())

        @block.sync
        def _(sp):
            def load(src, slot):
                sp.dma_start(raw[:, slot].rearrange("p a n -> p (a n)"), src).then_inc(raw_landed[slot], 16)

            for j in range(RAW_SLOTS):
                load(weights[j], j)
            with sp.Fori(1, G_END * HALVES // RAW_SLOTS) as q:
                for j in range(RAW_SLOTS):
                    sp.wait_ge(lo_ready, q * RAW_SLOTS + (j + 1 - RAW_SLOTS))
                    load(weights[q * RAW_SLOTS + j], j)
            for t in range(KT):
                sp.wait_ge(out_ready, t + 1)
                sp.dma_start(outT[t], main[:, t]).then_inc(stored, 16)
            sp.wait_ge(stored, 16 * KT)

        @block.gpsimd
        def _(pool):
            def load(src, slot):
                pool.dma_start(modchunk[:, slot].rearrange("p a n -> p (a n)"), src).then_inc(chunk_landed[slot], 16)

            def pairs(first, end):
                with pool.Fori(first, end) as q:
                    for j in range(2):
                        pool.wait_ge(acc_step, q * 4 + (2 * j - 2))
                        load(modb[q * 2 + j], j)

            pool.wait_ge(rows_done, G_K)
            for j in range(2):
                load(modb[j], j)
            pairs(1, M_O * HALVES // 2)
            for q in range(4):
                if q == 0:
                    pool.wait_ge(split_done, H_MIX0 + KT)
                part = slice(4 * q, 4 * q + 4)
                pool.dma_start(main[:, part], xT[part].rearrange("t p n -> p t n")).then_inc(res_landed, 16)
            pairs(M_O * HALVES // 2, M_END * HALVES // 2)

        @block.scalar
        def _(act):
            def hi(n, j, grp=0, free=True):
                slot = j % RAW_SLOTS
                act.wait_ge(raw_landed[slot], (n * 2 + (j // RAW_SLOTS + 1)) * 16)
                if grp is None:
                    act.wait_ge(p_used, 2 * (j - 2) + 2)
                elif free and j <= HALVES:
                    act.wait_ge(weights_used, (n - grp) * (HALVES - 1) + (j - 1))
                nc.scalar.copy(w_hi[:, j % 2], raw[:, slot]).then_inc(hi_ready, 1)

            def square(index, x, n):
                if index >= 2:
                    act.wait_ge(sq_summed, index - 1)
                nc.scalar.activation(tmp[:, index % 2, 0:n], x, ACT.Square).then_inc(squared, 1)

            def root(k, dst):
                act.wait_ge(var_ready, k)
                nc.scalar.activation(dst, dst, ACT.Sqrt).then_inc(rstd_ready, 1)

            def split(index, x, dst, bias=None):
                act.wait_ge(tile_ready, index + 1)
                if bias is None:
                    ins = nc.scalar.copy(dst, x)
                else:
                    ins = nc.scalar.activation(dst, x, ACT.Identity, bias=bias)
                ins.then_inc(split_hi, 1)

            def group(n, b, evac, ctx_banks=None):
                for s in range(HALVES - 1):
                    hi(n, s + 2)
                for m in range(GROUP):
                    act.wait_ge(bank_done, b * GROUP + (m + 1))
                    evac(m)
                if ctx_banks:
                    act.wait_ge(cbank_done, ctx_banks)
                hi(n, HALVES + 1)

            act.dma_start(vec[:], vectors).then_inc(vec_landed, 16)
            for q in range(4):
                part = slice(4 * q, 4 * q + 4)
                act.dma_start(main[:, part], xT[part].rearrange("t p n -> p t n")).then_inc(x_landed, 16)
            act.dma_start(ctx_t, ctxT.rearrange("t p n -> p t n")).then_inc(ctx_landed, 16)
            act.dma_start(rope, rope_in).then_inc(rope_landed, 16)
            act.dma_start(edges[:], edges_in).then_inc(rope_landed, 16)
            act.wait_ge(vec_landed, 16)
            nc.scalar.activation(cond_t[:].rearrange("p t v -> p (t v)"), vec[:, V_C:V_BM0], ACT.Tanh,
                                 scale=0.5).then_inc(cond_tanh, 1)
            act.wait_ge(cond_ready, 1)
            nc.scalar.copy(cond_split[:, :, :, 0], cond[:]).then_inc(cond_hi_ready, 1)
            act.wait_ge(sinks_ready, 1)
            nc.scalar.copy(sink_hi[:, :, 0], vec[:, V_SINK:V_ID]).then_inc(sinks_hi_ready, 1)
            def mod_unit_hi(cg, j):
                act.wait_ge(raw_landed[j % RAW_SLOTS], (cg * 2 + (j // RAW_SLOTS + 1)) * 16)
                if j >= RAW_SLOTS:
                    act.wait_ge(weights_used, cg * (HALVES - 1) + (j - RAW_SLOTS + 1))
                elif j == 2 and cg:
                    act.wait_ge(weights_used, cg * (HALVES - 1))
                nc.scalar.copy(mod_hi[j % RAW_SLOTS], raw[:, j % RAW_SLOTS]).then_inc(hi_ready, 1)

            def mod_square(cg, s):
                if cg not in range(1, 5):
                    return
                index = HALVES * (cg - 1) + s
                if index == 0:
                    act.wait_ge(x_landed, 64)
                if index == KT:
                    act.wait_ge(ctx_landed, 16)
                if index < KT:
                    square(index, main[:, index], SEQ)
                else:
                    square(index, ctx_t[:, index - KT], CTX)

            mod_unit_hi(0, 0)
            mod_unit_hi(0, 1)
            for cg in range(G_K):
                for s in range(HALVES - 1):
                    mod_unit_hi(cg, s + 2)
                    mod_square(cg, s)
                mod_unit_hi(cg, HALVES + 1)
                act.wait_ge(rows_done, cg + 1)
                if cg:
                    act.wait_ge(rows_turned, cg)
                nc.scalar.copy(mod_rows, ps[0:4, cg % 2]).then_inc(rows_ready, 1)
                mod_square(cg, HALVES - 1)
            root(1, rstd_x)
            root(2, rstd_c)
            for t in range(KT):
                split(H_X + 2 * t, main[:, t], h_hi[:, t], mod0_v[:, 0, t, 0:1])
                split(H_X + 2 * t + 1, ctx_t[:, t], hc_hi[:, t], mod0_v[:, 0, t, 1:2])

            def copy_to(dst):
                def evac(m):
                    nc.scalar.copy(dst(m), ps[:, m]).then_inc(bank_free, 1)
                return evac

            def swaps(index, b, view):
                for m in range(GROUP):
                    if not (isinstance(index, int) and index + m < 2):
                        act.wait_ge(roped, index + (m - 1))
                    act.wait_ge(bank_free, b * GROUP + (m + 1))
                    act.sem_inc(swap_begun, 1)
                    for p in range(0, P, 32):
                        q = p ^ 32
                        ins = nc.scalar.activation(tmp[q:q + 32, m % 2, 0:SEQ], view(m)[p:p + 32], ACT.Identity)
                    ins.then_inc(swapped, 1)

            group(G_K, B_K, copy_to(lambda m: keys[:, m]), GROUP)
            swaps(0, B_K, lambda m: keys[:, m])
            group(G_V, B_V, copy_to(lambda m: values[:, m]), GROUP + CTX_TILES)
            act.dma_start(dft_ch[:], dft_ch_in).then_inc(fft_landed, 16)
            act.dma_start(wf_sb[:], wf.rearrange("g p n -> p g n")).then_inc(fft_landed, 16)
            act.dma_start(dft_tok[:], dft_tok_in).then_inc(fft_landed, 16)
            with act.Fori(0, 3) as i:
                group(i + G_Q, i + B_Q, copy_to(lambda m: main[:, i * GROUP + (GROUP + m)]))
                swaps(i * GROUP + GROUP, i + B_Q, lambda m: main[:, i * GROUP + (GROUP + m)])
            group(G_F, B_F, copy_to(lambda m: main[:, m]))

            for g in range(FG):
                act.wait_ge(mixer_done, g + 1)
                nc.scalar.copy(mixer[:, g], ps[:, 4 + g, 0:2 * P]).then_inc(mixer_ready, 1)
            for g in range(FG + 2):
                if g < FG:
                    act.wait_ge(ft_done, g + 1)
                    if g >= 2:
                        act.wait_ge(bank_done, B_FFT * GROUP + g - 1)
                    pair = 2 * (g % 2) + 4
                    nc.scalar.copy(half_ft[:, g % 2].rearrange("p t n -> p (t n)"),
                                   ps_flat[:, pair * 512:(pair + 2) * 512]).then_inc(ft_ready, 1)
                if g >= 2:
                    act.wait_ge(bank_done, B_FFT * GROUP + g - 1)
                    nc.scalar.copy(main[:, g - 2], ps[:, g - 2]).then_inc(bank_free, 1)
            act.dma_start(ident[:], ident_in).then_inc(attn_landed, 16)
            act.dma_start(identb[:], identb_in).then_inc(attn_landed, 16)
            act.dma_start(masks[:], masks_in).then_inc(attn_landed, 16)

            def tanh_bank(b, ready, m):
                act.wait_ge(bank_done, b * GROUP + (m + 1))
                act.wait_ge(tile_ready, ready + (m - 1))
                nc.scalar.activation(tmp[:, m % 2, 0:SEQ], ps[:, m], ACT.Tanh, scale=0.5).then_inc(tanh_done, 1)

            def residual_squares(b, added, t0):
                for m in range(GROUP):
                    act.wait_ge(bank_free, b * GROUP + (m + 1))
                    act.wait_ge(sq_added, added + (m + 1))
                    nc.scalar.activation(tmp[:, m % 2, 0:SEQ], main[:, t0 + m], ACT.Square).then_inc(squared, 1)

            def piece(dst, src):
                nc.scalar.activation(dst, src, ACT.Identity).then_inc(piece_hi, 1)

            def keys_and_first_queries(i):
                piece(k_hi[:, 0:SEQ], keys[:, i])
                piece(k_hi[:, SEQ:], keys_c[:, i])
                piece(q_hi[:, 0], main[:, bass.ds(i * GQA + FG, GQA), 0:P])

            def attention(i, last=False):
                piece(v_hi[:, 0:BLOCKS], values[:, :, bass.ds(i * P, P)])
                piece(v_hi[:, BLOCKS:], values_c[:, :, bass.ds(i * P, P)])
                for k in range(STEPS + 2):
                    if k in UNIT_SLOTS:
                        hi(i + G_Z, UNIT_SLOTS.index(k) + 2)
                    if k in QUERY_SLOTS:
                        n = QUERY_SLOTS.index(k) + 1
                        if n >= 2:
                            act.wait_ge(scores_done, i * STEPS + GQA * (n - 1))
                        piece(q_hi[:, n % 2], main[:, bass.ds(i * GQA + FG, GQA), n * P:(n + 1) * P])
                    if 1 <= k <= STEPS:
                        cols = score_width(k - 1) - 1
                        act.wait_ge(turned, i * STEPS + k)
                        nc.scalar.copy(pt_hi[:, 0:cols], ps_flat[:, 6 * 512:6 * 512 + cols]).then_inc(pt_hi_ready, 1)
                    if k < STEPS:
                        width = score_width(k)
                        act.wait_ge(negmax_ready, i * STEPS + (k + 1))
                        nc.scalar.activation(probs[:, k % 2, 0:width], ps_flat[:, S_END - width:S_END], ACT.Exp,
                                             bias=stat[:, 1, k % 2:k % 2 + 1], scale=SCALE,
                                             accum_out=stat[:, 2, k % 2:k % 2 + 1]).then_inc(exp_done, 1)
                    if k == STEPS and not last:
                        act.wait_ge(scores_done, i * STEPS + STEPS)
                        keys_and_first_queries(i + 1)
                for m in range(GROUP):
                    tanh_bank(i + B_Z, i * GROUP + H_MIX0, m)
                hi(i + G_Z, HALVES + 1)

            keys_and_first_queries(0)
            with act.Fori(0, KV_HEADS - 1) as i:
                attention(i)
            attention(KV_HEADS - 1, last=True)

            for t in range(KT):
                split(H_MIX0 + t, main[:, t], h_hi[:, t])
            with act.Fori(0, 4) as i:
                for s in range(HALVES - 1):
                    hi(i + G_O, s + 2)
                act.wait_ge(bank_done, i * GROUP + (B_O + 1) * GROUP)
                hi(i + G_O, HALVES + 1)
                residual_squares(i + B_O, i * GROUP + SUM_0, i * GROUP)

            root(3, rstd[:])
            for t in range(KT):
                split(H_L1 + t, tmp[:, t % 2, 0:SEQ], h_hi[:, t], modv[:, 1, t:t + 1])
            with act.Fori(0, 4) as i:
                for s in range(HALVES - 1):
                    hi(i + G_U, s + 2)
                for m in range(GROUP):
                    act.wait_ge(bank_done, i * GROUP + (B_U * GROUP + m + 1))
                    act.wait_ge(ubuf_free, i * GROUP + (m + 1))
                    nc.scalar.copy(ubuf[:, m, PAD:PAD + SEQ], ps[:, m]).then_inc(bank_free, 1)
                hi(i + G_U, HALVES + 1)

            def pooled_hi(g, kt):
                act.wait_ge(ubuf_free, GROUP * (g + 1) + kt + 1)
                if g:
                    act.wait_ge(p_used, GROUP * (g - 1) + kt + 1)
                nc.scalar.copy(p_hi[:, kt], pooled[:, GROUP * g + kt]).then_inc(p_hi_ready, 1)

            for kt in range(GROUP):
                pooled_hi(0, kt)
            for g in range(GROUP):
                for half in range(2):
                    hi(G_GRP, 2 * g + half + 2, grp=None)
                    if g + 1 < GROUP:
                        pooled_hi(g + 1, 2 * half)
                        pooled_hi(g + 1, 2 * half + 1)
                for m in range(GROUP):
                    t = GROUP * g + m
                    act.wait_ge(p_used, GROUP * (g + 1))
                    nc.scalar.activation(pooled[:, t], ps[:, 4 * (g % 2) + m], ACT.Identity,
                                         scale=vec[:, V_LS + t:V_LS + t + 1]).then_inc(grp_free, 1)

            with act.Fori(0, 4) as i:
                for s in range(HALVES - 1):
                    hi(i + G_Z1, s + 2, grp=1)
                for m in range(GROUP):
                    tanh_bank(i + B_Z1, i * GROUP + H_MIX1, m)
                hi(i + G_Z1, HALVES + 1)
            for t in range(KT):
                split(H_MIX1 + t, pooled[:, t], h_hi[:, t])
            with act.Fori(0, 3) as i:
                for s in range(HALVES - 1):
                    hi(i + G_O1, s + 2, grp=1)
                act.wait_ge(bank_done, i * GROUP + (B_O1 + 1) * GROUP)
                hi(i + G_O1, HALVES + 1)
                residual_squares(i + B_O1, i * GROUP + SUM_1, i * GROUP)
            for s in range(HALVES - 2):
                hi(G_END - 1, s + 2, grp=1)
            residual_squares(B_O1 + 3, SUM_1 + 3 * GROUP, 3 * GROUP)
            root(4, rstd[:])

        @block.vector
        def _(dve):
            chain = Chain(dve, own)
            modv_flat = modv[:].rearrange("p a t -> p (a t)")

            def lo(n, j):
                dve.wait_ge(hi_ready, n * HALVES + (j + 1))
                nc.vector.tensor_tensor(w_lo[:, j % 2], raw[:, j % RAW_SLOTS], w_hi[:, j % 2].bitcast(F32),
                                        ALU.subtract).then_inc(lo_ready, 1)

            def job(cg, s):
                dve.wait_ge(chunk_landed[s % 2], (cg * GROUP + (s // 2 + 1)) * 16)
                for r in range(2):
                    kt = 2 * s + r
                    if kt:
                        dve.wait_ge(acc_step, cg * KT + kt)
                        ins = nc.vector.scalar_tensor_tensor(out=modacc[:], in0=modchunk[:, s % 2, r],
                                                             scalar=cond[:, kt, 0:1], in1=modacc[:],
                                                             op0=ALU.mult, op1=ALU.add)
                    else:
                        ins = nc.vector.tensor_scalar(modacc[:], modchunk[:, s % 2, r], cond[:, 0, 0:1], None,
                                                      ALU.mult)
                    ins.then_inc(acc_step, 1)

            def reduced(cg):
                dve.wait_ge(acc_reduced, cg + 1)
                nc.vector.tensor_tensor(modv_flat[:, bass.ds(cg * GROUP, GROUP)],
                                        ps[:, RED_BANK, RED_COL:RED_COL + GROUP],
                                        vec[:, bass.ds(cg * GROUP + V_BMB, GROUP)], ALU.add).then_inc(red_free, 1)

            def group(n, cg, finish, later=None, last=False):
                for s in range(HALVES - 1 if not last else HALVES - 2):
                    lo(n, s + 2)
                    if cg is not None:
                        if s == 0 and not (isinstance(cg, int) and cg == 0):
                            reduced(cg - 1)
                        job(cg, s)
                if cg is not None:
                    job(cg, HALVES - 1)
                finish()
                if not last:
                    lo(n, HALVES + 1)
                if later:
                    later()

            def variance(k, sums, dst, n):
                if k > 2:
                    dve.wait_ge(ssum_done, k - 2)
                if k > 1:
                    dve.wait_ge(var_ready, k - 1)
                chain.link(nc.vector.tensor_scalar(scratch[:, 0:n], sums, 1.0 / D, EPS, ALU.mult, ALU.add))
                nc.vector.reciprocal(dst, scratch[:, 0:n]).then_inc(var_ready, 1)

            def normed(x, dst, g, r):
                nc.vector.scalar_tensor_tensor(out=dst, in0=x, scalar=g, in1=r, op0=ALU.mult,
                                               op1=ALU.mult).then_inc(tile_ready, 1)

            def split(index, x, hi_part, dst, shift=None):
                dve.wait_ge(split_hi, index + 1)
                h = hi_part.bitcast(F32)
                if shift is None:
                    ins = nc.vector.tensor_tensor(dst, x, h, ALU.subtract)
                else:
                    ins = nc.vector.scalar_tensor_tensor(out=dst, in0=x, scalar=shift, in1=h, op0=ALU.add,
                                                         op1=ALU.subtract)
                ins.then_inc(split_done, 1)

            def rotate(index, m, x):
                dve.wait_ge(swapped, index + (m + 1))
                t = tmp[:, m % 2, 0:SEQ]
                nc.vector.tensor_tensor(t, t, rope[:, 1], ALU.mult)
                chain.link(nc.vector.tensor_tensor(x, x, rope[:, 0], ALU.mult))
                nc.vector.tensor_tensor(x, x, t, ALU.add).then_inc(roped, 1)

            def residual(b, t0, layer_gate):
                for m in range(GROUP):
                    dve.wait_ge(bank_done, b * GROUP + (m + 1))
                    t = bass.ds(t0 + m, 1)
                    nc.vector.scalar_tensor_tensor(out=main[:, t0 + m], in0=ps[:, m], scalar=modv[:, layer_gate, t],
                                                   in1=main[:, t0 + m], op0=ALU.mult,
                                                   op1=ALU.add).then_inc(bank_free, 1)

            def clear_sum():
                for half in range(2):
                    nc.vector.memset(ssum[:, half * CTX:(half + 1) * CTX], 0.0).then_inc(sq_added, 1)

            def add_squares(index, added):
                for m in range(GROUP):
                    dve.wait_ge(squared, index + (m + 1))
                    dve.wait_ge(sq_added, added + (m + 2))
                    nc.vector.tensor_tensor(ssum, ssum, tmp[:, m % 2, 0:SEQ], ALU.add).then_inc(sq_added, 1)

            def gate_mix(b, done, t0, buf):
                for m in range(GROUP):
                    dve.wait_ge(tanh_done, done + (m + 1))
                    t = tmp[:, m % 2, 0:SEQ]
                    nc.vector.scalar_tensor_tensor(out=t, in0=t, scalar=1.0, in1=ps[:, m], op0=ALU.add,
                                                   op1=ALU.mult).then_inc(bank_free, 1)
                    dve.wait_ge(bank_free, b * GROUP + (m + 1))
                    nc.vector.scalar_tensor_tensor(out=buf[:, t0 + m], in0=buf[:, t0 + m], scalar=0.5, in1=t,
                                                   op0=ALU.mult, op1=ALU.mult).then_inc(tile_ready, 1)

            nc.vector.memset(ones, 1.0).then_inc(ones_ready, 1)
            nc.vector.memset(sink_hi[:].bitcast(F32), 0.0)
            nc.vector.memset(sink_lo[:].bitcast(F32), 0.0)
            dve.wait_ge(cond_tanh, 1)
            c_in = vec[:, V_C:V_BM0].rearrange("p (t v) -> p t v", v=2)
            chain.link(nc.vector.scalar_tensor_tensor(out=cond[:], in0=cond_t[:], scalar=1.0, in1=c_in,
                                                      op0=ALU.add, op1=ALU.mult))
            nc.vector.tensor_scalar(cond[:], cond[:], 0.5, None, ALU.mult).then_inc(cond_ready, 1)
            sinks = vec[:, V_SINK:V_ID]
            nc.vector.tensor_scalar(sinks, sinks, 1.0 / SCALE, None, ALU.mult).then_inc(sinks_ready, 1)
            dve.wait_ge(cond_hi_ready, 1)
            nc.vector.tensor_tensor(cond_split[:, :, :, 1], cond[:], cond_split[:, :, :, 0].bitcast(F32),
                                    ALU.subtract).then_inc(cond_split_ready, 1)
            dve.wait_ge(sinks_hi_ready, 1)
            chain.link(nc.vector.tensor_tensor(sink_lo[:, :, 0], sinks, sink_hi[:, :, 0].bitcast(F32), ALU.subtract))

            def mod_unit_lo(cg, j):
                dve.wait_ge(hi_ready, cg * HALVES + (j + 1))
                nc.vector.tensor_tensor(mod_lo[j % RAW_SLOTS], raw[:, j % RAW_SLOTS],
                                        mod_hi[j % RAW_SLOTS].bitcast(F32), ALU.subtract).then_inc(lo_ready, 1)

            mod_unit_lo(0, 0)
            mod_unit_lo(0, 1)
            for cg in range(G_K):
                for s in range(HALVES):
                    mod_unit_lo(cg, s + 2)
                if cg == 5:
                    dve.wait_ge(sq_summed, 2 * KT)
                    variance(1, ps[:, 5], rstd_x, SEQ)
                    variance(2, ps[:, 6, 0:CTX], rstd_c, CTX)

            dve.wait_ge(rows_turned, G_K)
            mod0_flat = mod0_v[:].rearrange("p a t v -> p (a t v)")
            chain.link(nc.vector.tensor_reduce(mod0_flat, ps[:, MOD_BANK, 0:8 * KT].rearrange("p (a b) -> p a b", b=2),
                                               AX.X, ALU.add))
            chain.link(nc.vector.tensor_tensor(mod0_flat, mod0_flat, vec[:, V_BM0:V_BMB], ALU.add))
            for v in range(2):
                ins = nc.vector.scalar_tensor_tensor(out=gain[:, v], in0=mod0_v[:, 1, :, v], scalar=1.0,
                                                     in1=vec[:, V_G0:V_G1], op0=ALU.add, op1=ALU.mult)
            chain.link(ins)
            dve.wait_ge(rstd_ready, 2)

            def normed_pair(t):
                normed(main[:, t], main[:, t], gain[:, 0, t:t + 1], rstd_x)
                normed(ctx_t[:, t], ctx_t[:, t], gain[:, 1, t:t + 1], rstd_c)

            normed_pair(0)
            for t in range(KT):
                if t + 1 < KT:
                    normed_pair(t + 1)
                split(H_X + 2 * t, main[:, t], h_hi[:, t], h_lo[:, t], mod0_v[:, 0, t, 0:1])
                split(H_X + 2 * t + 1, ctx_t[:, t], hc_hi[:, t], hc_lo[:, t], mod0_v[:, 0, t, 1:2])

            def finish_keys():
                for m in range(GROUP):
                    dve.wait_ge(cbank_done, m + 1)
                    nc.vector.tensor_copy(keys_c[:, m], ps[:, 4 + m, 0:CTX]).then_inc(cbank_free, 1)

            def rotate_keys():
                dve.wait_ge(rope_landed, 32)
                for m in range(GROUP):
                    rotate(0, m, keys[:, m])

            def finish_values():
                for m in range(CTX_TILES):
                    dve.wait_ge(cbank_done, GROUP + m + 1)
                    nc.vector.tensor_copy(values_c[:, m], ps[:, 4 + m]).then_inc(cbank_free, 1)

            group(G_K, M_K, finish_keys, rotate_keys)
            group(G_V, M_V, finish_values)
            per = GROUP
            with dve.Fori(0, 3) as i:
                chain.loop(i, per)

                def rotate_queries():
                    for m in range(GROUP):
                        rotate(i * GROUP + GROUP, m, main[:, i * GROUP + (GROUP + m)])

                group(i + G_Q, i + M_Q, lambda: None, rotate_queries)
            chain.end(3)
            group(G_F, M_F, lambda: None)
            reduced(M_FFT - 1)
            for s in range(HALVES):
                job(M_FFT, s)

            def piece(count, dst, src, hi_part):
                dve.wait_ge(piece_hi, count)
                nc.vector.tensor_tensor(dst, src, hi_part.bitcast(F32), ALU.subtract).then_inc(piece_ready, 1)

            def keys_and_first_queries(i):
                piece(i * PIECES + 1, k_lo[:, 0:SEQ], keys[:, i], k_hi[:, 0:SEQ])
                piece(i * PIECES + 2, k_lo[:, SEQ:], keys_c[:, i], k_hi[:, SEQ:])
                piece(i * PIECES + 3, q_lo[:, 0], main[:, bass.ds(i * GQA + FG, GQA), 0:P], q_hi[:, 0])

            def attention(i, last=False):
                for k in range(STEPS + 2):
                    par = k % 2
                    if k >= 2:
                        n, j = divmod(k - 2, GQA)
                        dve.wait_ge(pv_done, i * STEPS + (k - 1))
                        nc.vector.tensor_scalar(main[:, i * GQA + (FG + j), n * P:(n + 1) * P], ps[:, 7, P:2 * P],
                                                1.0, None, ALU.mult).then_inc(y_done, 1)
                    if k < STEPS:
                        width = score_width(k)
                        dve.wait_ge(scores_done, i * STEPS + (k + 1))
                        chain.link(nc.vector.tensor_reduce(stat[:, 0, par:par + 1], ps_flat[:, S_END - width:S_END],
                                                           AX.X, ALU.max))
                        nc.vector.tensor_scalar(stat[:, 1, par:par + 1], stat[:, 0, par:par + 1], -SCALE, None,
                                                ALU.mult).then_inc(negmax_ready, 1)
                    if k == 0:
                        piece(i * PIECES + 4, v_lo[:, 0:BLOCKS], values[:, :, bass.ds(i * P, P)], v_hi[:, 0:BLOCKS])
                        piece(i * PIECES + 5, v_lo[:, BLOCKS:], values_c[:, :, bass.ds(i * P, P)], v_hi[:, BLOCKS:])
                        reduced(i + (M_Z - 1))
                    if k in UNIT_SLOTS:
                        lo(i + G_Z, UNIT_SLOTS.index(k) + 2)
                    if k in QUERY_SLOTS:
                        n = QUERY_SLOTS.index(k) + 1
                        piece(i * PIECES + (5 + n), q_lo[:, n % 2],
                              main[:, bass.ds(i * GQA + FG, GQA), n * P:(n + 1) * P], q_hi[:, n % 2])
                    if 1 <= k <= STEPS:
                        cols = score_width(k - 1) - 1
                        dve.wait_ge(pt_hi_ready, i * STEPS + k)
                        nc.vector.tensor_tensor(pt_lo[:, 0:cols], ps_flat[:, 6 * 512:6 * 512 + cols],
                                                pt_hi[:, 0:cols].bitcast(F32), ALU.subtract).then_inc(pt_ready, 1)
                    if k < STEPS:
                        dve.wait_ge(exp_done, i * STEPS + (k + 1))
                        chain.link(nc.vector.reciprocal(stat[:, 3, par:par + 1], stat[:, 2, par:par + 1]))
                        p = probs[:, par, 0:width - 1]
                        nc.vector.tensor_scalar(p, p, stat[:, 3, par:par + 1], None,
                                                ALU.mult).then_inc(probs_ready, 1)
                    if k in JOB_SLOTS:
                        job(i + M_Z, JOB_SLOTS.index(k))
                    if k == STEPS and not last:
                        keys_and_first_queries(i + 1)
                dve.wait_ge(y_done, i * STEPS + STEPS)
                gate_mix(i + B_Z, i * GROUP, i * GROUP, main)
                lo(i + G_Z, HALVES + 1)

            keys_and_first_queries(0)
            with dve.Fori(0, KV_HEADS - 1) as i:
                chain.loop(i, 2 * STEPS)
                attention(i)
            chain.end(KV_HEADS - 1)
            attention(KV_HEADS - 1, last=True)

            clear_sum()
            for t in range(KT):
                split(H_MIX0 + t, main[:, t], h_hi[:, t], h_lo[:, t])
            with dve.Fori(0, 4) as i:
                def finish_out():
                    dve.wait_ge(res_landed, 16 * 4)
                    residual(i + B_O, i * GROUP, 0)

                group(i + G_O, i + M_O, finish_out, lambda: add_squares(i * GROUP + SQ_0, i * GROUP + SUM_0))
            reduced(M_GRP - 1)
            dve.wait_ge(red_free, M_GRP)
            variance(3, ps[:, 5], rstd[:], SEQ)
            chain.link(nc.vector.scalar_tensor_tensor(out=gain[:, 2], in0=modv[:, 2], scalar=1.0,
                                                      in1=vec[:, V_G1:V_GF], op0=ALU.add, op1=ALU.mult))
            dve.wait_ge(rstd_ready, 3)
            normed(main[:, 0], tmp[:, 0, 0:SEQ], gain[:, 2, 0:1], rstd[:])
            for t in range(KT):
                if t + 1 < KT:
                    if t:
                        dve.wait_ge(split_done, H_L1 + t)
                    normed(main[:, t + 1], tmp[:, (t + 1) % 2, 0:SEQ], gain[:, 2, t + 1:t + 2], rstd[:])
                split(H_L1 + t, tmp[:, t % 2, 0:SEQ], h_hi[:, t], h_lo[:, t], modv[:, 1, t:t + 1])

            for m in range(GROUP):
                nc.vector.memset(ubuf[:, m], 0.0).then_inc(ubuf_free, 1)

            def pool_tile(g, m):
                w = POOL_WINDOWS[g]
                t = GROUP * g + m
                dve.wait_ge(bank_free, (B_U + g) * GROUP + m + 1)
                dve.wait_ge(ubuf_free, GROUP + t)
                src, size = ubuf[:, m], WIDE
                step, buf = 1, 0
                while step < w:
                    size -= step
                    chain.link(nc.vector.tensor_tensor(tmp[:, buf, 0:size], src[:, 0:size],
                                                       src[:, step:step + size], ALU.add))
                    src, step, buf = tmp[:, buf], 2 * step, 1 - buf
                win = src[:, PAD - w // 2:PAD - w // 2 + SEQ]
                ends = win.rearrange("p (a b) -> p a b", b=PAD)[:, 0:SEQ // PAD:SEQ // PAD - 1]
                chain.link(nc.vector.tensor_tensor(ends, ends, edges[:, g], ALU.mult))
                nc.vector.scalar_tensor_tensor(out=pooled[:, t], in0=win, scalar=1.0 / w, in1=ubuf[:, m, PAD:PAD + SEQ],
                                               op0=ALU.mult, op1=ALU.subtract).then_inc(ubuf_free, 1)

            for g in range(GROUP):
                for s in range(HALVES):
                    lo(G_U + g, s + 2)
                    if g and s < GROUP:
                        pool_tile(g - 1, s)

            def pooled_lo(g, kt):
                dve.wait_ge(p_hi_ready, GROUP * g + kt + 1)
                nc.vector.tensor_tensor(p_lo[:, kt], pooled[:, GROUP * g + kt], p_hi[:, kt].bitcast(F32),
                                        ALU.subtract).then_inc(p_ready, 1)

            for kt in range(GROUP):
                pooled_lo(0, kt)
            for g in range(GROUP):
                for half in range(2):
                    lo(G_GRP, 2 * g + half + 2)
                    if g + 1 < GROUP:
                        pooled_lo(g + 1, 2 * half)
                        pooled_lo(g + 1, 2 * half + 1)
                    if g < 2:
                        pool_tile(GROUP - 1, 2 * g + half)
                    else:
                        for s in range(2):
                            job(M_GRP, 4 * (g - 2) + 2 * half + s)

            def group_z1(i):
                group(i + G_Z1, None, lambda: gate_mix(i + B_Z1, (i + KV_HEADS) * GROUP, i * GROUP, pooled))

            with dve.Fori(0, 4) as i:
                group_z1(i)
            reduced(M_GRP)
            for t in range(KT):
                split(H_MIX1 + t, pooled[:, t], h_hi[:, t], h_lo[:, t])
            clear_sum()
            dve.wait_ge(red_free, M_END)
            with dve.Fori(0, 3) as i:
                group(i + G_O1, None, lambda: residual(i + B_O1, i * GROUP, 3),
                      lambda: add_squares(i * GROUP + SQ_1, i * GROUP + SUM_1))
            group(G_END - 1, None, lambda: residual(B_O1 + 3, 3 * GROUP, 3),
                  lambda: add_squares(SQ_1 + 3 * GROUP, SUM_1 + 3 * GROUP), last=True)
            variance(4, ps[:, 5], rstd[:], SEQ)
            dve.wait_ge(rstd_ready, 4)
            for t in range(KT):
                nc.vector.scalar_tensor_tensor(out=main[:, t], in0=main[:, t], scalar=vec[:, V_GF + t:V_GF + t + 1],
                                               in1=rstd[:], op0=ALU.mult, op1=ALU.mult).then_inc(out_ready, 1)

        @block.tensor
        def _(pe):
            def mm(out, lhsT, rhs, start, stop):
                return nc.tensor.matmul(out, lhsT, rhs, start=start, stop=stop, skip_group_check=True)

            def three(out, a_hi, a_lo, b_hi, b_lo, start, stop):
                mm(out, a_hi, b_hi, start, False)
                mm(out, a_hi, b_lo, False, False)
                return mm(out, a_lo, b_hi, False, stop)

            def unit_bank(s, m, x_hi=h_hi, x_lo=h_lo, n=SEQ, bank=0):
                for r in range(2):
                    kt, cols = 2 * s + r, slice(m * P, (m + 1) * P)
                    ins = three(ps[:, bank + m, 0:n], w_hi[:, s % 2, r, cols], w_lo[:, s % 2, r, cols],
                                x_hi[:, kt], x_lo[:, kt], kt == 0, kt == KT - 1)
                return ins

            def token_bank(s, m, x_hi=h_hi, x_lo=h_lo, bank=0):
                for r in range(2):
                    kt, toks = 2 * s + r, slice(m * P, (m + 1) * P)
                    ins = three(ps[:, bank + m], x_hi[:, kt, toks], x_lo[:, kt, toks],
                                w_hi[:, s % 2, r], w_lo[:, s % 2, r], kt == 0, kt == KT - 1)
                return ins

            def unit(n, b, s, m, make=unit_bank, signal=None):
                if m == 0:
                    pe.wait_ge(lo_ready, n * HALVES + (s + 1))
                if s == 0 and not (isinstance(b, int) and b == 0):
                    pe.wait_ge(bank_free, b * GROUP + (m + 1 - GROUP))
                ins = make(s, m)
                if s == HALVES - 1:
                    ins.then_inc(bank_done, 1)
                elif m == GROUP - 1:
                    ins.then_inc(weights_used, 1)

            def reduce(cg):
                pe.wait_ge(acc_step, cg * KT + KT)
                if not (isinstance(cg, int) and cg == 0):
                    pe.wait_ge(red_free, cg)
                for m in range(GROUP):
                    ins = mm(ps[:, RED_BANK, RED_COL + m:RED_COL + m + 1], modacc[:, m * P:(m + 1) * P], ones[:, 0:1],
                             m == 0, True)
                ins.then_inc(acc_reduced, 1)

            def group(n, b, split_base, cg=None, make=unit_bank):
                for s in range(HALVES):
                    if split_base is not None:
                        pe.wait_ge(split_done, split_base + 2 * s + 2)
                    for m in range(GROUP):
                        unit(n, b, s, m, make)
                    if s == 0 and cg is not None:
                        reduce(cg)

            def sum_squares(added):
                pe.wait_ge(sq_added, added)
                mm(ps[:, 5], ones, ssum, True, True).then_inc(ssum_done, 1)

            def mod_square(cg, s):
                if cg not in range(1, 5):
                    return
                index = HALVES * (cg - 1) + s
                t, bank, n = (index, 5, SEQ) if index < KT else (index - KT, 6, CTX)
                pe.wait_ge(squared, index + 1)
                mm(ps[:, bank, 0:n], ones, tmp[:, index % 2, 0:n], t == 0, t == KT - 1).then_inc(sq_summed, 1)

            pe.wait_ge(ones_ready, 1)
            pe.wait_ge(cond_split_ready, 1)
            for cg in range(G_K):
                for s in range(HALVES):
                    pe.wait_ge(lo_ready, cg * HALVES + s + 1)
                    for r in range(2):
                        kt = 2 * s + r
                        stationary = cond_split[:, kt].rearrange("p v h -> p (v h)")
                        mm(ps[0:4, cg % 2], stationary, mod_hi[s % RAW_SLOTS][:, r], kt == 0, False)
                        ins = mm(ps[0:4, cg % 2], stationary, mod_lo[s % RAW_SLOTS][:, r], False, kt == KT - 1)
                    ins.then_inc(weights_used if s < HALVES - 1 else rows_done, 1)
                    if s < HALVES - 1:
                        mod_square(cg, s)
                pe.wait_ge(rows_ready, cg + 1)
                for m in range(GROUP):
                    at = (cg * GROUP + m) * 4
                    ins = mm(ps[:, MOD_BANK, at:at + 4], mod_rows[:, m * P:(m + 1) * P],
                             vec[0:4, V_ID:V_END], m == 0, True)
                ins.then_inc(rows_turned, 1)
                mod_square(cg, HALVES - 1)

            for s in range(HALVES):
                pe.wait_ge(split_done, 4 * s + 4)
                for m in range(GROUP):
                    if m == 0:
                        pe.wait_ge(lo_ready, G_K * HALVES + s + 1)
                    ins = unit_bank(s, m)
                    if s == HALVES - 1:
                        ins.then_inc(bank_done, 1)
                    ins = unit_bank(s, m, hc_hi, hc_lo, CTX, 4)
                    if s == HALVES - 1:
                        ins.then_inc(cbank_done, 1)
                    elif m == GROUP - 1:
                        ins.then_inc(weights_used, 1)

            pe.wait_ge(cbank_free, GROUP)
            for s in range(HALVES):
                pe.wait_ge(lo_ready, G_V * HALVES + s + 1)
                for m in range(GROUP):
                    if s == 0:
                        pe.wait_ge(bank_free, B_V * GROUP + m + 1 - GROUP)
                    ins = token_bank(s, m)
                    if s == HALVES - 1:
                        ins.then_inc(bank_done, 1)
                for m in range(CTX_TILES):
                    ins = token_bank(s, m, hc_hi, hc_lo, 4)
                    if s == HALVES - 1:
                        ins.then_inc(cbank_done, 1)
                if s < HALVES - 1:
                    ins.then_inc(weights_used, 1)
                if s == 0:
                    reduce(M_V - 1)
            with pe.Fori(0, 3) as i:
                group(i + G_Q, i + B_Q, None, i + (M_Q - 1))
            group(G_F, B_F, None, M_F - 1)

            pe.wait_ge(fft_landed, 48)
            pe.wait_ge(cbank_free, GROUP + CTX_TILES)
            pe.wait_ge(red_free, M_F)
            for g in range(FG):
                for c in range(2):
                    ins = mm(ps[:, 4 + g, c * P:(c + 1) * P], dft_ch[:, c], wf_sb[:, g], c == 0, True)
                ins.then_inc(mixer_done, 1)
            pe.wait_ge(mixer_ready, FG)
            reduce(M_FFT - 1)
            pe.wait_ge(bank_free, (B_F + 1) * GROUP)
            for g in range(FG + 1):
                if g < FG:
                    if g == 1:
                        pe.wait_ge(red_free, M_FFT)
                    if g >= 2:
                        pe.wait_ge(ft_ready, g - 1)
                    for t in range(BLOCKS):
                        ins = mm(ps[:, 4 + 2 * (g % 2) + t // 2, 256 * (t % 2):256 * (t % 2) + 256],
                                 main[:, g, t * P:(t + 1) * P], mixer[:, g], t % 2 == 0, True)
                    ins.then_inc(ft_done, 1)
                if g >= 1:
                    f = g - 1
                    pe.wait_ge(ft_ready, f + 1)
                    for c in range(2):
                        for t in range(BLOCKS):
                            ins = mm(ps[:, f], half_ft[:, f % 2, t, c * P:(c + 1) * P], dft_tok[:, c, t],
                                     c == 0 and t == 0, c == 1 and t == BLOCKS - 1)
                    ins.then_inc(bank_done, 1)

            pe.wait_ge(attn_landed, 48)

            def scores(i, k):
                n, j = divmod(k, GQA)
                first, end = block_tiles(n)
                if j == 0:
                    pe.wait_ge(piece_ready, i * PIECES + (PIECES_BEFORE if n == 0 else 5 + n))
                if k:
                    pe.wait_ge(exp_done, i * STEPS + k)
                qh, ql = q_hi[:, n % 2, j], q_lo[:, n % 2, j]
                at, window, past = 512 - (end - first) * P, slice(first * P, end * P), slice(SEQ, SEQ + CTX)
                three(ps[:, 4, at:512], qh, ql, k_hi[:, window], k_lo[:, window], True, False)
                if n > first:
                    mm(ps[:, 4, at:at + P], identb[:], masks[:, 0], False, False)
                if end > n + 1:
                    mm(ps[:, 4, 512 - P:512], identb[:], masks[:, 1], False, True)
                three(ps[:, 5, 0:CTX], qh, ql, k_hi[:, past], k_lo[:, past], True, True)
                head = i * GQA + j
                mm(ps[:, 5, CTX:CTX + 2], ones_r[:], sink_hi[:, head], False, False)
                mm(ps[:, 5, CTX:CTX + 2], ones_r[:], sink_lo[:, head], False, True).then_inc(scores_done, 1)

            def turn(i, k):
                pe.wait_ge(probs_ready, i * STEPS + (k + 1))
                if k >= 1:
                    pe.wait_ge(y_done, i * STEPS + k)
                for t in range(score_width(k) // P):
                    ins = nc.tensor.transpose(ps_flat[:, 6 * 512 + t * P:6 * 512 + (t + 1) * P],
                                              probs[:, k % 2, t * P:(t + 1) * P], ident[:])
                ins.then_inc(turned, 1)

            def attend(i, k):
                first, end = block_tiles(k // GQA)
                tiles = list(range(first, end)) + [BLOCKS, BLOCKS + 1]
                pe.wait_ge(pt_ready, i * STEPS + (k + 1))
                if k == 0:
                    pe.wait_ge(piece_ready, i * PIECES + 5)
                    pe.wait_ge(red_free, i + M_Z)
                for c, t in enumerate(tiles):
                    cols = slice(c * P, (c + 1) * P)
                    ins = three(ps[:, 7, P:2 * P], v_hi[:, t], v_lo[:, t], pt_hi[:, cols], pt_lo[:, cols], c == 0,
                                c == len(tiles) - 1)
                ins.then_inc(pv_done, 1)

            def attention(i):
                step = 0
                for k, count in enumerate(BANK_STEPS):
                    if k >= 2:
                        attend(i, k - 2)
                    if k < STEPS:
                        scores(i, k)
                    if 0 < k <= STEPS:
                        turn(i, k - 1)
                    for _ in range(count):
                        unit(i + G_Z, i + B_Z, *divmod(step, GROUP))
                        step += 1
                    if k == 0:
                        reduce(i + (M_Z - 1))
                pe.wait_ge(y_done, i * STEPS + STEPS)

            with pe.Fori(0, KV_HEADS) as i:
                attention(i)

            with pe.Fori(0, 4) as i:
                group(i + G_O, i + B_O, H_MIX0, i + (M_O - 1))
            reduce(M_GRP - 1)
            sum_squares(SUM_1)
            with pe.Fori(0, 4) as i:
                group(i + G_U, i + B_U, H_L1)

            pe.wait_ge(red_free, M_GRP)
            for g in range(GROUP):
                for kt in range(GROUP):
                    s = 2 * g + kt // 2
                    pe.wait_ge(p_ready, GROUP * g + kt + 1)
                    pe.wait_ge(lo_ready, G_GRP * HALVES + s + 1)
                    for m in range(GROUP):
                        if kt == 0 and g < 2:
                            pe.wait_ge(bank_free, B_Z1 * GROUP + m + 1 - GROUP)
                        if kt == 0 and g >= 2:
                            pe.wait_ge(grp_free, GROUP * (g - 2) + m + 1)
                        cols = slice(m * P, (m + 1) * P)
                        ins = three(ps[:, 4 * (g % 2) + m], w_hi[:, s % 2, kt % 2, cols], w_lo[:, s % 2, kt % 2, cols],
                                    p_hi[:, kt], p_lo[:, kt], kt == 0, kt == GROUP - 1)
                    ins.then_inc(p_used, 1)
            pe.wait_ge(grp_free, GROUP * (GROUP - 1))

            with pe.Fori(0, 4) as i:
                group(i + G_Z1, i + B_Z1, None)
            pe.wait_ge(grp_free, GROUP * GROUP)
            reduce(M_GRP)
            with pe.Fori(0, 4) as i:
                group(i + G_O1, i + B_O1, H_MIX1)
            sum_squares(SUM_END)


def stream(w, col_groups):
    parts = [w[:, g * COLS:(g + 1) * COLS].reshape(-1, 2, P, COLS).transpose(0, 2, 1, 3).reshape(-1, P, 2 * COLS)
             for g in col_groups]
    return np.concatenate(parts)


def per_partition(v):
    return v.reshape(-1, P).T


def rope_tables():
    pairs = P // 4
    inv = 1.0 / 10000.0 ** (np.arange(pairs) / pairs)
    tok = np.arange(SEQ)
    angle = np.concatenate([np.outer(inv, pos) for pos in (tok // 64, tok // 64, tok % 64, tok % 64)])
    sign = np.repeat([-1.0, 1.0, -1.0, 1.0], pairs)[:, None]
    return np.stack([np.cos(angle), sign * np.sin(angle)], axis=1).astype(np.float32)


def constants():
    bf16 = mybir.dt.np(BF16)
    q = np.arange(P)[:, None]
    k = np.arange(P)[None, :]
    masks = np.stack([np.where(k >= q, 0.0, MASKED), np.where(k <= q, 0.0, MASKED)], axis=1)
    tok = 2 * np.pi / SEQ * (np.outer(np.arange(SEQ), np.arange(SEQ)) % SEQ)
    norm = 1.0 / np.sqrt(SEQ * P)
    dft_tok = np.stack([np.cos(tok) * norm, -np.sin(tok) * norm]).reshape(2, BLOCKS, P, SEQ).transpose(2, 0, 1, 3)
    ch = 2 * np.pi / P * (np.outer(np.arange(P), np.arange(P)) % P)
    dft_ch = np.stack([np.cos(ch), np.sin(ch)], axis=1)
    edges = np.ones((GROUP, 2, PAD))
    for g, w in enumerate(POOL_WINDOWS):
        for e, first in enumerate((0, SEQ - PAD)):
            for c in range(PAD):
                t = first + c
                edges[g, e, c] = w / (min(t - w // 2 + w, SEQ) - max(t - w // 2, 0))
    f32 = np.float32
    return {
        "ident": np.eye(P, dtype=f32), "identb": np.eye(P).astype(bf16),
        "masks": masks.astype(bf16), "rope": rope_tables(), "dft_tok": dft_tok.astype(f32),
        "dft_ch": dft_ch.astype(f32), "edges": np.broadcast_to(edges, (P,) + edges.shape).astype(f32),
    }


def layouts(x, c, ctx, c_ctx, l0_norm, l0_w_mod, l0_b_mod, l0_w_in, l0_sink, l0_w_f, l0_w_out,
            l1_norm, l1_w_mod, l1_b_mod, l1_w_in, l1_w_grp, l1_scale, l1_w_out, final_norm):
    mixed = np.roll(np.arange(KT), FG)
    q0, k0, v0, f0, z0 = 0, 3, 4, 5, 6
    in0 = stream(l0_w_in, [k0, v0, q0, q0 + 1, q0 + 2, f0, z0 + 3, z0, z0 + 1, z0 + 2])
    out0 = stream(l0_w_out.reshape(KT, P, D)[mixed].reshape(D, D), range(4))
    in1 = stream(l1_w_in, range(4))
    grp = np.concatenate([stream(l1_w_grp[g], [0]) for g in range(GROUP)])
    gate1 = stream(l1_w_in, range(4, 8))
    out1 = stream(l1_w_out, range(4))
    cond = np.stack([per_partition(c[0]), per_partition(c_ctx)], axis=2).reshape(P, -1)
    b0 = per_partition(l0_b_mod)
    sink = np.zeros((P, HEADS), np.float32)
    sink[0] = l0_sink
    unit_rows = np.eye(P, 4, dtype=np.float32)
    vectors = np.concatenate([
        cond, np.repeat(b0[:, 0:2 * KT], 2, axis=1), b0[:, 2 * KT:], per_partition(l1_b_mod),
        per_partition(l0_norm), per_partition(l1_norm), per_partition(final_norm), per_partition(l1_scale), sink,
        unit_rows,
    ], axis=1)
    return {
        "weights": np.concatenate([stream(l0_w_mod, range(8)), in0, out0, in1, grp, gate1, out1]),
        "modb": np.concatenate([stream(l0_w_mod, range(8, 12)), stream(l1_w_mod, range(12))]),
        "xT": x[0].T.reshape(KT, P, SEQ), "ctxT": ctx[0].T.reshape(KT, P, CTX),
        "vectors": vectors, "wf": l0_w_f,
    }


def kernel(**inputs):
    import concourse.bacc as bacc
    from concourse.bass_utils import run_bass_kernel_spmd

    nc = bacc.Bacc("TRN2", target_bir_lowering=False, num_devices=1)
    arrays, args = {}, []
    for name, a in {**layouts(**{k: np.asarray(v) for k, v in inputs.items()}), **constants()}.items():
        arrays[f"in_{name}"] = np.ascontiguousarray(a)
        args.append(nc.dram_tensor(f"in_{name}", a.shape, mybir.dt.from_np(a.dtype), kind="ExternalInput").ap())
    out = nc.dram_tensor("out", (KT, P, SEQ), F32, kind="ExternalOutput").ap()
    build(nc, *args, out)
    result = run_bass_kernel_spmd(nc, [arrays], core_ids=[0]).results[0]["out"]
    return np.ascontiguousarray(np.asarray(result).reshape(D, SEQ).T)[None]
```
